# Optimizing a Trainium2 kernel written in Bass

```python
import math
import jax, jax.numpy as jnp
from jax import lax
import numpy as np

D_MODEL = 1024
BATCH = 1
SEQ = 512
DEPTH = 1
DEC_BATCH = 1
DEC_SEQ = 64
PAST_LEN = 1024

CHUNK = 64
N_Q_HEADS = 8
N_KV_HEADS = 2
GQA = N_Q_HEADS // N_KV_HEADS
HEAD_DIM = 64
WINDOW = 128
WINDOW_BLOCKS = WINDOW // CHUNK
BAND = (WINDOW_BLOCKS + 1) * CHUNK
ATT_CACHE = min(WINDOW, PAST_LEN)
ROPE_DIM = HEAD_DIM // 4
ROPE_THETA = 500000.0
ATT_WIDTH = N_Q_HEADS * HEAD_DIM
KV_WIDTH = N_KV_HEADS * HEAD_DIM
SSM_GROUP = 16
SSM_WIDTH = D_MODEL // 2
N_SSM_GROUPS = SSM_WIDTH // SSM_GROUP
SSM_STATE = 64
MIX_WIDTH = ATT_WIDTH + SSM_WIDTH
IN_WIDTH = ATT_WIDTH + 2 * KV_WIDTH + SSM_WIDTH
N_MEM = 256
CA_HEADS = 4
CA_HEAD_DIM = 128
CA_WIDTH = CA_HEADS * CA_HEAD_DIM
N_EXPERT_GROUPS = 4
EXPERTS_PER_GROUP = 8
N_EXPERTS = N_EXPERT_GROUPS * EXPERTS_PER_GROUP
TOP_K = 2
D_EXPERT = 512
MOE_BLOCK = 256
EPS = 1e-6
NEG = -1e30
F32 = jnp.float32

kernel_name = 'hymba_style_streaming_swa_s5_hmoe_step'

def rms_norm(x, g):
    xf = x.astype(F32)
    y = xf * lax.rsqrt(jnp.mean(xf * xf, axis=-1, keepdims=True) + EPS)
    return (y * g.astype(F32)).astype(x.dtype)

def partial_rope(x, pos):
    half = ROPE_DIM // 2
    inv = ROPE_THETA ** (-jnp.arange(0, ROPE_DIM, 2, dtype=F32) / ROPE_DIM)
    ang = pos.astype(F32)[:, None] * inv[None, :]
    cos = jnp.cos(ang)[:, None, :]
    sin = jnp.sin(ang)[:, None, :]
    xr = x[..., :ROPE_DIM].astype(F32)
    x1, x2 = xr[..., :half], xr[..., half:]
    rot = jnp.concatenate([x1 * cos - x2 * sin, x2 * cos + x1 * sin], axis=-1)
    return jnp.concatenate([rot.astype(x.dtype), x[..., ROPE_DIM:]], axis=-1)

def sink_attention(q, k, v, mask, sink):
    s = jnp.einsum('...qhgd,...khd->...hgqk', q.astype(F32), k.astype(F32)) * (HEAD_DIM ** -0.5)
    s = jnp.where(mask[..., None, None, :, :], s, NEG)
    sk = sink.astype(F32).reshape(N_KV_HEADS, GQA, 1, 1)
    m = jnp.maximum(jnp.max(s, axis=-1, keepdims=True), sk)
    p = jnp.exp(s - m)
    den = jnp.sum(p, axis=-1, keepdims=True) + jnp.exp(sk - m)
    o = jnp.einsum('...hgqk,...khd->...qhgd', p / den, v.astype(F32))
    return o.astype(q.dtype)

def window_attn_prompt(q, k, v, sink):
    B, S = q.shape[:2]
    nb = S // CHUNK
    qb = q.reshape(B, nb, CHUNK, N_KV_HEADS, GQA, HEAD_DIM)
    pad = ((0, 0), (WINDOW_BLOCKS * CHUNK, 0), (0, 0), (0, 0))
    kb = jnp.pad(k, pad).reshape(B, nb + WINDOW_BLOCKS, CHUNK, N_KV_HEADS, HEAD_DIM)
    vb = jnp.pad(v, pad).reshape(B, nb + WINDOW_BLOCKS, CHUNK, N_KV_HEADS, HEAD_DIM)
    kband = jnp.concatenate([kb[:, j:j + nb] for j in range(WINDOW_BLOCKS + 1)], axis=2)
    vband = jnp.concatenate([vb[:, j:j + nb] for j in range(WINDOW_BLOCKS + 1)], axis=2)
    src = jnp.arange(nb)[:, None] + jnp.arange(WINDOW_BLOCKS + 1)[None, :] - WINDOW_BLOCKS
    valid = jnp.repeat(src >= 0, CHUNK, axis=1)
    mask = jnp.broadcast_to(valid[:, None, :], (nb, CHUNK, BAND))
    o = sink_attention(qb, kband, vband, mask, sink)
    return o.reshape(B, S, ATT_WIDTH)

def window_attn_sample(q, k, v, ck, cv, sink):
    B, L = q.shape[:2]
    kk = jnp.concatenate([ck.astype(k.dtype), k], axis=1)
    vv = jnp.concatenate([cv.astype(v.dtype), v], axis=1)
    mask = jnp.ones((L, kk.shape[1]), dtype=bool)
    o = sink_attention(q.reshape(B, L, N_KV_HEADS, GQA, HEAD_DIM), kk, vv, mask, sink)
    return o.reshape(B, L, ATT_WIDTH)

def _lin_rec(e1, e2):
    a1, b1 = e1
    a2, b2 = e2
    return a1 * a2, a2 * b1 + b2

def s5_branch(u, h0, lam_re, lam_im, log_dt, b_re, b_im, c_re, c_im, d, w_glu, b_glu):
    B, L, _ = u.shape
    ug = u.reshape(B, L, N_SSM_GROUPS, SSM_GROUP).astype(F32)
    lam = lax.complex(lam_re.astype(F32), lam_im.astype(F32))
    dt = jnp.exp(log_dt.astype(F32))[:, None]
    lam_bar = jnp.exp(lam * dt)
    bmat = lax.complex(b_re.astype(F32), b_im.astype(F32))
    b_bar = ((lam_bar - 1.0) / lam)[..., None] * bmat
    cmat = lax.complex(c_re.astype(F32), c_im.astype(F32))
    blk = CHUNK if L % CHUNK == 0 else L
    nblk = L // blk
    us = ug.reshape(B, nblk, blk, N_SSM_GROUPS, SSM_GROUP).transpose(1, 0, 2, 3, 4)

    def step(h, u_blk):
        bu = jnp.einsum('gnp,bsgp->bsgn', b_bar, u_blk.astype(jnp.complex64))
        bu = bu.at[:, 0].add(lam_bar * h)
        a = jnp.broadcast_to(lam_bar, bu.shape)
        _, hs = lax.associative_scan(_lin_rec, (a, bu), axis=1)
        y = jnp.einsum('gpn,bsgn->bsgp', cmat, hs).real
        return hs[:, -1], y

    h_last, ys = lax.scan(step, h0, us)
    y = ys.transpose(1, 0, 2, 3, 4).reshape(B, L, N_SSM_GROUPS, SSM_GROUP) + d.astype(F32) * ug
    g = jax.nn.gelu(y)
    out = g * jax.nn.sigmoid(jnp.einsum('bsgp,gpq->bsgq', g, w_glu.astype(F32)) + b_glu.astype(F32))
    return out.reshape(B, L, SSM_WIDTH).astype(u.dtype), h_last

def token_mixer(x, pos, h0, ck, cv, g_mix, w_in, g_q, g_k, sink, ssm_p, g_ao, g_so, w_out):
    B, L, _ = x.shape
    hin = rms_norm(x, g_mix) @ w_in
    o1 = ATT_WIDTH
    o2 = o1 + KV_WIDTH
    o3 = o2 + KV_WIDTH
    q = hin[..., :o1].reshape(B, L, N_Q_HEADS, HEAD_DIM)
    k = hin[..., o1:o2].reshape(B, L, N_KV_HEADS, HEAD_DIM)
    v = hin[..., o2:o3].reshape(B, L, N_KV_HEADS, HEAD_DIM)
    u = hin[..., o3:]
    q = partial_rope(rms_norm(q, g_q), pos)
    k = partial_rope(rms_norm(k, g_k), pos)
    if ck is None:
        att = window_attn_prompt(q, k, v, sink)
    else:
        att = window_attn_sample(q, k, v, ck, cv, sink)
    ssm, h_last = s5_branch(u, h0, *ssm_p)
    mixed = jnp.concatenate([rms_norm(att, g_ao), rms_norm(ssm, g_so)], axis=-1) @ w_out
    return x + mixed, k, v, h_last

def memory_kv(mem, g_mem, w_ck, w_cv, g_k):
    B, M = mem.shape[:2]
    m = rms_norm(mem, g_mem)
    k = rms_norm((m @ w_ck).reshape(B, M, CA_HEADS, CA_HEAD_DIM), g_k)
    v = (m @ w_cv).reshape(B, M, CA_HEADS, CA_HEAD_DIM)
    return k, v

def cross_attention(x, mk, mv, g_x, w_cq, g_q, w_co):
    B, L = x.shape[:2]
    q = rms_norm((rms_norm(x, g_x) @ w_cq).reshape(B, L, CA_HEADS, CA_HEAD_DIM), g_q)
    s = jnp.einsum('bqhd,bkhd->bhqk', q.astype(F32), mk.astype(F32)) * (CA_HEAD_DIM ** -0.5)
    p = jax.nn.softmax(s, axis=-1)
    o = jnp.einsum('bhqk,bkhd->bqhd', p, mv.astype(F32)).astype(x.dtype).reshape(B, L, CA_WIDTH)
    return o @ w_co

def hier_moe(x, w_rg, b_rg, w_re, b_re, w_gate, w_up, w_down):
    shp = x.shape
    h = x.reshape(-1, D_MODEL)
    T = h.shape[0]
    lg = (h @ w_rg).astype(F32) + b_rg.astype(F32)
    pg = jax.nn.softmax(lg, axis=-1)
    pg_top, grp = lax.top_k(pg, 1)
    le = ((h @ w_re).astype(F32) + b_re.astype(F32)).reshape(T, N_EXPERT_GROUPS, EXPERTS_PER_GROUP)
    le_sel = jnp.einsum('tn,tne->te', jax.nn.one_hot(grp[:, 0], N_EXPERT_GROUPS, dtype=F32), le)
    pe = jax.nn.softmax(le_sel, axis=-1)
    w_top, i_top = lax.top_k(pe, TOP_K)
    gate = pg_top * w_top / jnp.sum(w_top, axis=-1, keepdims=True)
    eid = grp * EXPERTS_PER_GROUP + i_top
    n_pairs = T * TOP_K
    flat_e = eid.reshape(-1).astype(jnp.int32)
    flat_w = gate.reshape(-1)
    flat_tok = jnp.repeat(jnp.arange(T, dtype=jnp.int32), TOP_K)
    order = jnp.argsort(flat_e)
    se = flat_e[order]
    counts = jnp.bincount(flat_e, length=N_EXPERTS)
    padded = (counts + MOE_BLOCK - 1) // MOE_BLOCK * MOE_BLOCK
    pad_end = jnp.cumsum(padded)
    pad_start = pad_end - padded
    start = jnp.cumsum(counts) - counts
    dest = pad_start[se] + jnp.arange(n_pairs, dtype=jnp.int32) - start[se]
    n_blocks = (n_pairs + N_EXPERTS * (MOE_BLOCK - 1)) // MOE_BLOCK + 1
    rows = n_blocks * MOE_BLOCK
    row_tok = jnp.full((rows,), T, jnp.int32).at[dest].set(flat_tok[order])
    row_w = jnp.zeros((rows,), F32).at[dest].set(flat_w[order])
    block_e = jnp.minimum(jnp.searchsorted(pad_end, jnp.arange(n_blocks) * MOE_BLOCK, side='right'), N_EXPERTS - 1)
    xb = jnp.concatenate([h, jnp.zeros((1, D_MODEL), h.dtype)], axis=0)[row_tok].reshape(n_blocks, MOE_BLOCK, D_MODEL)

    def expert_block(args):
        xe, e = args
        return (jax.nn.silu(xe @ w_gate[e]) * (xe @ w_up[e])) @ w_down[e]

    yb = lax.map(expert_block, (xb, block_e)).reshape(rows, D_MODEL)
    out = jnp.zeros((T + 1, D_MODEL), F32).at[row_tok].add(yb.astype(F32) * row_w[:, None])[:T]
    return out.astype(x.dtype).reshape(shp)

def setup_inputs(seed: int = 0) -> dict:
    key = jax.random.key(seed)
    ks = iter(jax.random.split(key, 64))

    def nrm(shape, scale):
        return jax.random.normal(next(ks), shape, F32) * scale

    def gain(shape):
        return 1.0 + nrm(shape, 0.02)

    G, N, P = N_SSM_GROUPS, SSM_STATE, SSM_GROUP
    return {
        'x_prompt': nrm((BATCH, SEQ, D_MODEL), 1.0),
        'x_sample': nrm((DEC_BATCH, DEC_SEQ, D_MODEL), 1.0),
        'cache_attn_k': nrm((DEPTH, DEC_BATCH, ATT_CACHE, N_KV_HEADS, HEAD_DIM), 1.0),
        'cache_attn_v': nrm((DEPTH, DEC_BATCH, ATT_CACHE, N_KV_HEADS, HEAD_DIM), 1.0),
        'state_ssm_re': nrm((DEPTH, DEC_BATCH, G, N), 0.1),
        'state_ssm_im': nrm((DEPTH, DEC_BATCH, G, N), 0.1),
        'cache_mem_k': nrm((DEPTH, DEC_BATCH, N_MEM, CA_HEADS, CA_HEAD_DIM), 1.0),
        'cache_mem_v': nrm((DEPTH, DEC_BATCH, N_MEM, CA_HEADS, CA_HEAD_DIM), 1.0),
        'mem_prompt': nrm((BATCH, N_MEM, D_MODEL), 1.0),
        'norm_mix': gain((DEPTH, D_MODEL)),
        'w_in': nrm((DEPTH, D_MODEL, IN_WIDTH), D_MODEL ** -0.5),
        'q_norm': gain((DEPTH, HEAD_DIM)),
        'k_norm': gain((DEPTH, HEAD_DIM)),
        'attn_sink': nrm((DEPTH, N_Q_HEADS), 0.5),
        'ssm_lambda_re': -0.5 + nrm((DEPTH, G, N), 0.01),
        'ssm_lambda_im': math.pi * jnp.arange(N, dtype=F32)[None, None, :] + nrm((DEPTH, G, N), 0.01),
        'ssm_log_dt': jax.random.uniform(next(ks), (DEPTH, G), F32, math.log(1e-3), math.log(1e-1)),
        'ssm_b_re': nrm((DEPTH, G, N, P), (2.0 * P) ** -0.5),
        'ssm_b_im': nrm((DEPTH, G, N, P), (2.0 * P) ** -0.5),
        'ssm_c_re': nrm((DEPTH, G, P, N), (2.0 * N) ** -0.5),
        'ssm_c_im': nrm((DEPTH, G, P, N), (2.0 * N) ** -0.5),
        'ssm_d': nrm((DEPTH, G, P), 1.0),
        'ssm_w_glu': nrm((DEPTH, G, P, P), P ** -0.5),
        'ssm_b_glu': nrm((DEPTH, G, P), 0.02),
        'norm_attn_out': gain((DEPTH, ATT_WIDTH)),
        'norm_ssm_out': gain((DEPTH, SSM_WIDTH)),
        'w_out': nrm((DEPTH, MIX_WIDTH, D_MODEL), MIX_WIDTH ** -0.5),
        'norm_cross': gain((DEPTH, D_MODEL)),
        'norm_mem': gain((DEPTH, D_MODEL)),
        'w_cq': nrm((DEPTH, D_MODEL, CA_WIDTH), D_MODEL ** -0.5),
        'w_ck': nrm((DEPTH, D_MODEL, CA_WIDTH), D_MODEL ** -0.5),
        'w_cv': nrm((DEPTH, D_MODEL, CA_WIDTH), D_MODEL ** -0.5),
        'cq_norm': gain((DEPTH, CA_HEAD_DIM)),
        'ck_norm': gain((DEPTH, CA_HEAD_DIM)),
        'w_co': nrm((DEPTH, CA_WIDTH, D_MODEL), CA_WIDTH ** -0.5),
        'norm_ffn': gain((DEPTH, D_MODEL)),
        'w_router_group': nrm((DEPTH, D_MODEL, N_EXPERT_GROUPS), D_MODEL ** -0.5),
        'b_router_group': nrm((DEPTH, N_EXPERT_GROUPS), 0.01),
        'w_router_expert': nrm((DEPTH, D_MODEL, N_EXPERTS), D_MODEL ** -0.5),
        'b_router_expert': nrm((DEPTH, N_EXPERTS), 0.01),
        'w_e_gate': nrm((DEPTH, N_EXPERTS, D_MODEL, D_EXPERT), D_MODEL ** -0.5),
        'w_e_up': nrm((DEPTH, N_EXPERTS, D_MODEL, D_EXPERT), D_MODEL ** -0.5),
        'w_e_down': nrm((DEPTH, N_EXPERTS, D_EXPERT, D_MODEL), D_EXPERT ** -0.5),
    }

def reference(x_prompt, x_sample, cache_attn_k, cache_attn_v, state_ssm_re, state_ssm_im,
              cache_mem_k, cache_mem_v, mem_prompt,
              norm_mix, w_in, q_norm, k_norm, attn_sink,
              ssm_lambda_re, ssm_lambda_im, ssm_log_dt, ssm_b_re, ssm_b_im, ssm_c_re, ssm_c_im,
              ssm_d, ssm_w_glu, ssm_b_glu, norm_attn_out, norm_ssm_out, w_out,
              norm_cross, norm_mem, w_cq, w_ck, w_cv, cq_norm, ck_norm, w_co,
              norm_ffn, w_router_group, b_router_group, w_router_expert, b_router_expert,
              w_e_gate, w_e_up, w_e_down):
    yp, ys = x_prompt, x_sample
    Bp, Lp = yp.shape[:2]
    Ls = ys.shape[1]
    pos_p = jnp.arange(Lp, dtype=jnp.int32)
    pos_s = PAST_LEN + jnp.arange(Ls, dtype=jnp.int32)
    kp_l, vp_l, hpr_l, hpi_l, mkp_l, mvp_l = [], [], [], [], [], []
    ks_l, vs_l, hsr_l, hsi_l = [], [], [], []
    for l in range(DEPTH):
        ssm_p = (ssm_lambda_re[l], ssm_lambda_im[l], ssm_log_dt[l], ssm_b_re[l], ssm_b_im[l],
                 ssm_c_re[l], ssm_c_im[l], ssm_d[l], ssm_w_glu[l], ssm_b_glu[l])
        h0p = jnp.zeros((Bp, N_SSM_GROUPS, SSM_STATE), jnp.complex64)
        h0s = lax.complex(state_ssm_re[l].astype(F32), state_ssm_im[l].astype(F32))
        yp, kp, vp, hp = token_mixer(yp, pos_p, h0p, None, None, norm_mix[l], w_in[l], q_norm[l], k_norm[l],
                                     attn_sink[l], ssm_p, norm_attn_out[l], norm_ssm_out[l], w_out[l])
        ys, kn, vn, hn = token_mixer(ys, pos_s, h0s, cache_attn_k[l], cache_attn_v[l], norm_mix[l], w_in[l],
                                     q_norm[l], k_norm[l], attn_sink[l], ssm_p, norm_attn_out[l],
                                     norm_ssm_out[l], w_out[l])
        mkp, mvp = memory_kv(mem_prompt, norm_mem[l], w_ck[l], w_cv[l], ck_norm[l])
        yp = yp + cross_attention(yp, mkp, mvp, norm_cross[l], w_cq[l], cq_norm[l], w_co[l])
        ys = ys + cross_attention(ys, cache_mem_k[l], cache_mem_v[l], norm_cross[l], w_cq[l], cq_norm[l], w_co[l])
        yp = yp + hier_moe(rms_norm(yp, norm_ffn[l]), w_router_group[l], b_router_group[l], w_router_expert[l],
                           b_router_expert[l], w_e_gate[l], w_e_up[l], w_e_down[l])
        ys = ys + hier_moe(rms_norm(ys, norm_ffn[l]), w_router_group[l], b_router_group[l], w_router_expert[l],
                           b_router_expert[l], w_e_gate[l], w_e_up[l], w_e_down[l])
        kp_l.append(kp[:, Lp - ATT_CACHE:])
        vp_l.append(vp[:, Lp - ATT_CACHE:])
        hpr_l.append(hp.real)
        hpi_l.append(hp.imag)
        mkp_l.append(mkp)
        mvp_l.append(mvp)
        ks_l.append(kn)
        vs_l.append(vn)
        hsr_l.append(hn.real)
        hsi_l.append(hn.imag)
    return (yp, ys,
            jnp.stack(kp_l), jnp.stack(vp_l), jnp.stack(hpr_l), jnp.stack(hpi_l),
            jnp.stack(mkp_l), jnp.stack(mvp_l),
            jnp.stack(ks_l), jnp.stack(vs_l), jnp.stack(hsr_l), jnp.stack(hsi_l))


_drawn_inputs = setup_inputs


def setup_inputs(seed=0):
    import zlib

    import numpy as np

    out = dict(_drawn_inputs(seed))
    spreads = {}
    factors = {'q_norm': 3.674,
     'k_norm': 3.069,
     'attn_sink': 64.0,
     'ssm_lambda_re': 15.674,
     'ssm_b_glu': 6.357,
     'norm_attn_out': 3.067,
     'norm_ssm_out': 2.775,
     'norm_cross': 8.0,
     'norm_mem': 2.732,
     'cq_norm': 8.0,
     'ck_norm': 2.762,
     'b_router_group': 33.457,
     'b_router_expert': 19.497,
     'cache_attn_k': 8.0,
     'cache_attn_v': 8.0,
     'norm_ffn': 8.0}
    for name, (base, spread) in spreads.items():
        noise = np.random.default_rng([zlib.crc32(name.encode()), seed]).standard_normal(out[name].shape)
        drawn = base * np.exp(spread * noise) if base else spread * noise
        out[name] = __import__('jax').numpy.asarray(drawn.astype(out[name].dtype))
    for name, factor in factors.items():
        out[name] = (out[name] * factor).astype(out[name].dtype)
    return out
```

```python
import math

import numpy as np

DM, SEQ, DEC, PAST = 1024, 512, 64, 1024
NTOK = SEQ + DEC
P = 128
T = 5
HD, NQ, NKV = 64, 8, 2
ROPE = 16
NG, SG, SN = 32, 16, 64
NPAIR = NG // 2
L = 8
NCH_P, NCH_S = SEQ // L, DEC // L
NCH = NCH_P + NCH_S
CAH, CAD, NMEM = 4, 128, 256
NEG_, NEXP, EPG = 4, 32, 8
FE = 512
CAP = 64
N_OVF = 17
NBLK = NEXP + N_OVF
EPS = 1e-6
ROWS = [P, P, P, P, DEC]
TOK0 = [0, 128, 256, 384, 512]
KCOL = [0, 128, 256, 384, 640]
VIDX = [0, 1, 2, 3, 5]
PHYS = [1, 2, 0]
UROWS = [slice(0, P)] * 4 + [slice(DEC, P)]
UNITS = [(0, 7), (7, 14), (14, 16), (16, 23), (23, 30), (30, 32)]
MAGIC = 12582912.0
RT_EG, RT_D, RT_G1, RT_G2 = 185, 470, 480, 485

def half_rows(t, h):
    return slice(0, P) if t < 4 else slice(DEC * h, DEC * h + DEC)


INS = ['x_prompt', 'x_sample', 'cache_attn_k', 'cache_attn_v', 'state_ssm_re', 'state_ssm_im',
       'cache_mem_k', 'cache_mem_v', 'mem_prompt', 'norm_mix', 'w_in', 'q_norm', 'k_norm', 'attn_sink',
       'ssm_lambda_re', 'ssm_lambda_im', 'ssm_log_dt', 'ssm_b_re', 'ssm_b_im', 'ssm_c_re', 'ssm_c_im',
       'ssm_d', 'ssm_w_glu', 'ssm_b_glu', 'norm_attn_out', 'norm_ssm_out', 'w_out', 'norm_cross',
       'norm_mem', 'w_cq', 'w_ck', 'w_cv', 'cq_norm', 'ck_norm', 'w_co', 'norm_ffn', 'w_router_group',
       'b_router_group', 'w_router_expert', 'b_router_expert', 'w_e_gate', 'w_e_up', 'w_e_down']
OUTS = [('y_prompt', (1, SEQ, DM)), ('y_sample', (1, DEC, DM)),
        ('attn_k_prompt', (1, 1, 128, 2, 64)), ('attn_v_prompt', (1, 1, 128, 2, 64)),
        ('ssm_re_prompt', (1, 1, NG, SN)), ('ssm_im_prompt', (1, 1, NG, SN)),
        ('mem_k_prompt', (1, 1, NMEM, CAH, CAD)), ('mem_v_prompt', (1, 1, NMEM, CAH, CAD)),
        ('attn_k_sample', (1, 1, DEC, 2, 64)), ('attn_v_sample', (1, 1, DEC, 2, 64)),
        ('ssm_re_sample', (1, 1, NG, SN)), ('ssm_im_sample', (1, 1, NG, SN))]


def constants():
    ident = np.eye(P, dtype=np.float32)
    tri = np.triu(np.ones((P, P), np.float32), 1)
    inv = 500000.0 ** (-np.arange(0, ROPE, 2, dtype=np.float32) / ROPE)
    rope = np.zeros((P, T, 2, 16), np.float32)
    for t in range(T):
        pos = (TOK0[t] + np.arange(P)) if t < 4 else (PAST + np.arange(P))
        ang = (pos.astype(np.float32)[:, None] * inv[None, :].astype(np.float32)).astype(np.float32)
        c, s = np.cos(ang), np.sin(ang)
        rope[:, t, 0] = np.concatenate([c, c], 1)
        rope[:, t, 1] = np.concatenate([-s, s], 1)
    mask = np.zeros((P, P + 2 * P), np.float32)
    for b in (0, 64):
        mask[b, 0:64] = 1.0
        mask[b + 1, 64:128] = 1.0
        mask[b, P + 192:P + 256] = -1e30
        mask[b + 1, P:P + 64] = -1e30
    row = np.concatenate([np.arange(4, 0, -1), np.arange(8, 0, -1), 64 * np.arange(1, 9),
                          64 * np.arange(NEXP), 64 * (31 - np.arange(NEXP)), np.arange(N_OVF)])
    row = np.broadcast_to(row.astype(np.float32)[None], (P, row.size))
    return {'c_ident': ident, 'c_tri': tri, 'c_rope': rope.reshape(P, -1), 'c_mask': mask,
            'c_row': np.ascontiguousarray(row)}


CONSTS = constants()


def build(nc, A):
    import concourse.bass as bass
    import concourse.mybir as mybir
    from concourse.alu_op_type import AluOpType as ALU
    from contextlib import ExitStack
    F32, BF16, I32 = mybir.dt.float32, mybir.dt.bfloat16, mybir.dt.int32
    ACT, AX = mybir.ActivationFunctionType, mybir.AxisListType

    with ExitStack() as ctx:
        def sb(name, shape, dt=F32):
            return ctx.enter_context(nc.sbuf_tensor(name, shape, dt))

        def sem(name):
            return ctx.enter_context(nc.semaphore(name))

        u_dram = nc.dram_tensor("u_scratch", [NTOK, 512], F32).ap()
        slots_in = nc.dram_tensor("slots_in", [NBLK * CAP, DM], F32).ap()
        slots_out = nc.dram_tensor("slots_out", [NBLK * CAP, DM], F32).ap()

        slot = [sb(f"slot{j}", [P, 12288]) for j in range(3)]
        x = sb("x", [P, T, DM])
        wide = sb("wide", [P, 4608])
        att = sb("att", [P, 4480])

        def view(t, off, *dims):
            n = int(np.prod(dims))
            v = t[:, off:off + n]
            if len(dims) == 1:
                return v
            names = "abcdef"[:len(dims)]
            return v.rearrange(f"p ({' '.join(names)}) -> p {' '.join(names)}", **dict(zip(names, dims)))

        xT = view(wide, 0, 8, NTOK)
        vt = view(att, 0, 6, 128)
        qT = view(att, 768, 4, NTOK)
        kT = view(att, 3072, 2, 704)
        w_in = view(slot[0], 0, 8, 1280)
        usb = view(slot[0], 10240, 512)
        qk = view(slot[0], 10752, 640)
        sq = view(slot[0], 11392, 640)
        kdup = view(slot[0], 12032, 4, 64)
        x_sq = view(slot[0], 10240, DM)
        uc = view(slot[0], 0, 8, 512)
        yc = uc
        ucg = view(slot[0], 6400, NG, P)
        rot = view(slot[0], 0, 2, NPAIR * NCH)
        finrow = view(slot[0], 2304, 512)
        U = view(slot[0], 4096, 32 * NCH)
        Z = U
        H = view(slot[0], 6400, NG, NCH + 1)
        Htmp = view(slot[0], 6400, 2, NPAIR * NCH)
        Bst = view(slot[0], 8736, 2, NPAIR, NCH)
        Y = view(slot[0], 8736, 32 * NCH)
        atile = view(slot[0], 11040, 512)
        a_sq = view(slot[0], 11552, 512)
        w_cv = view(slot[0], 0, 8, 512)
        w_cq = view(slot[0], 4096, 8, 512)
        w_co = view(slot[0], 8192, 4, DM)
        WB = view(slot[1], 0, 2, NPAIR, P)
        GLU = view(slot[1], 0, NG, P)
        Wt = view(slot[1], 4096, 2, NPAIR, P)
        M = view(slot[1], 8192, NG, P)
        maskf = view(slot[1], 8192, 3 * P)
        trif = view(slot[1], 8576, P)
        smrow = view(slot[1], 9216, 1060)
        wbtmp = view(slot[1], 10240, 2048)
        vtmp = view(slot[1], 0, 1024)
        w_out_a = view(slot[1], 4096, 4, DM)
        w_out_s = view(slot[1], 0, 4, DM)
        w_ck = view(slot[1], 8192, 8, 512)
        V = view(slot[2], 0, NG, 144)
        Trot = view(slot[2], 4608, 2, NPAIR, NCH)
        R8 = view(slot[2], 6912, NPAIR, NCH)
        CS = view(slot[2], 6912, 2, NG, SG)
        Bb = view(slot[2], 8576, 2, NPAIR, SG)
        Braw = view(slot[2], 9088, 2, NPAIR, SG)
        Craw = view(slot[2], 9600, 2, 4, 2, 64)
        Kt = view(slot[2], 10624, 2, 4, P)
        BbS = view(slot[2], 9600, NG, SG)
        powS = view(slot[2], 11648, 2, NG, 9)
        pooltmp = view(slot[2], 4608, 2304)
        powr = view(slot[2], 9088, 2, NPAIR, 8)
        Prob = view(slot[2], 8192, 8, 256)
        PT = view(slot[2], 10240, 16, P)
        memx = view(slot[2], 0, 2, DM)
        memT = view(slot[2], 2048, 8, NMEM)
        mkt = [view(slot[2], 4096, 512), view(slot[2], 4608, 512)]
        cmk = view(slot[2], 5120, 2, 512)
        mem_sq = view(slot[2], 6144, DM)
        gck = view(slot[2], 7168, CAD)
        mksq = view(slot[2], 7296, 512)
        mkT = view(att, 0, CAH, 512)
        mv = view(att, 2048, 4, 512)
        x1T = view(wide, 0, 8, P)
        qc = view(wide, 1024, 512)
        qcT = view(wide, 1536, 4, P)
        cP = view(wide, 2048, 4, 256)
        cPT = view(wide, 3072, 8, P)
        oT = view(wide, 4096, 4, P)
        h3 = [view(wide, 0, DM), view(wide, 1024, DM), view(wide, 2048, DM), view(att, 3072, DM), view(wide, 3072, DM)]
        x2T = view(wide, 3072, 8, P)
        gffn = view(att, 0, DM)
        xg = [view(wide, 0, DM), view(wide, 1024, DM)]
        xgT = [view(wide, 2048, 8, CAP), view(wide, 2560, 8, CAP)]
        act1 = view(wide, 3072, 256)
        hact = view(wide, 3328, 256)
        hT = view(wide, 3584, 2, P)
        yb = [view(wide, 3840, 512), view(att, 0, 512)]
        yg = [[view(slot[0], 2048 * t, DM), view(slot[0], 2048 * t + 1024, DM)] for t in range(5)]

        ident = sb("ident", [P, P])
        wr = view(att, 4096, 8, 36)
        brt = view(att, 4384, 36)
        rt = view(att, 1024, 1280)
        hotb = att[:, 2304:2384].bitcast(BF16)
        crow = view(att, 2400, 101)
        rtmp = view(att, 2504, 544)
        maskb = sb("maskb", [P, 3 * P], BF16)
        trib = sb("trib", [P, 2 * P], BF16)
        rope = sb("rope", [P, T, 2, 16])
        gqk = sb("gqk", [P, 2, 64])
        gcol = sb("gcol", [P, 42])
        sinkr = sb("sinkr", [P, 2, 8])
        tiny = sb("tiny", [P, 192])
        ssm_s = sb("ssm_s", [P, 24, NPAIR])
        powj = sb("powj", [P, 2, NPAIR, 9])
        Db = sb("Db", [P, 2, NG])
        fin = sb("fin", [P, 4, NPAIR])
        zero = sb("zero", [P, 256])
        idx = sb("idx", [P, 10], I32)
        ovf = sb("ovf", [P, N_OVF + 1], I32)
        rs_v, rs_y, rs_t = (sb(n, [P, 16]) for n in ("rs_v", "rs_y", "rs_t"))
        mixT = xT
        g_mix, g_cross, g_mem = gcol[:, 0:8], gcol[:, 8:16], gcol[:, 16:24]
        g_ao, g_so, g_cq = gcol[:, 24:28], gcol[:, 28:32], gcol[:, 32:33]
        g_ffn = gcol[:, 34:42]

        bank = [ctx.enter_context(nc.psum_tensor(f"bank{b}", [P, 512], F32)) for b in range(8)]

        names = """ld_ident ld_const ld_gain ld_win0 ld_win1 ld_x0 ld_x1 ld_x2 ld_x3 ld_x4 ld_ssm ld_c ld_b ld_glu
        ld_cache ld_wout ld_wco ld_wc ld_wcq ld_wcv ld_mem ld_wr cst ssx xt_ps xt_sb proj_ps proj_sb u_sent
        u_stored qk_ready qk_ps qkt_sb kout sm_ps c_ps c_sb wb_ready wt_ps wt_sb k_ps k_sb m_ready
        uc_ld u_ps u_sb b_ps b_sb h_ready fin_ps fin_sb fin_out y_ps y_sb z_ps z_sb glu_done yt_ps
        yt_sb ssy yn my_ps my_sb s_ps nmax expd p_ps pt_sb o_ps a_ready ssa a_norm at_ps at_sb wo_ps
        x1 mt_ps mt_sb ssm_m mk_ps mk_sb mkn mkT_ps mkT_sb mv_ps mv_sb mem_out ssc cq_ps cq_sb cqn
        cqT_ps cqT_sb cs_ps cmax cexp cpn cp_ps cpt_sb co_ps co_sb cw_ps x2 ssf h3T_ps h3T_sb lg_ps
        oh_ready cnt_ps slots_ready zero_done sc_done0 sc_done1 xg_ld0 xg_ld1 xgt_ps xgt_sb silu
        hact_ready ht_ps ht_sb y_ready y_out0 y_out1 lg0 lg1 lg2 ldn0 ldn1 ldn2 gu_used dn_used v_w
        v_go gath0 gath1 gath2 gath3 gath4 out_st dve_step bb_ready gated x3 asked answered rms y_more
        cleared sm ssm_made ucg ssm_act pool_step pow_ready h3a ld_wout2""".split()
        S = {n: sem(n) for n in names}

        block = ctx.enter_context(nc.Block())

        @block.sync
        def _(sp):
            def ld(dst, src, s):
                sp.dma_start(dst, src).then_inc(S[s], 16)

            ld(ident[:, :], A['c_ident'], 'ld_ident')
            ld(x[:, 0, :], A['x_prompt'][0, 0:128, :], 'ld_x0')
            ld(gcol[:, 0:8], A['norm_mix'][0].rearrange("(p k) -> p k", p=P), 'ld_gain')
            wv = A['w_in'][0].rearrange("(p k) n -> p k n", k=8)
            ld(w_in[:, 0:2, :], wv[:, 0:2, :], 'ld_win0')
            ld(w_in[:, 2:4, :], wv[:, 2:4, :], 'ld_win0')
            ld(w_in[:, 4:6, :], wv[:, 4:6, :], 'ld_win1')
            ld(w_in[:, 6:8, :], wv[:, 6:8, :], 'ld_win1')
            ld(x[:, 1, :], A['x_prompt'][0, 128:256, :], 'ld_x1')
            ld(x[:, 2, :], A['x_prompt'][0, 256:384, :], 'ld_x2')
            ld(x[:, 3, :], A['x_prompt'][0, 384:512, :], 'ld_x3')
            ld(x[0:DEC, 4, :], A['x_sample'][0], 'ld_x4')
            for t in range(T):
                r = ROWS[t]
                sp.wait_ge(S['u_sent'], t + 1)
                ld(u_dram[TOK0[t]:TOK0[t] + r, :], usb[0:r, :], 'u_stored')
                if t == 4:
                    sp.wait_ge(S['qk_ready'], 4)
                    ld(A['attn_k_prompt'][0, 0].rearrange("s h d -> s (h d)"), qk[:, 512:640], 'kout')
                    ld(A['attn_v_prompt'][0, 0].rearrange("s h d -> s (h d)"), vt[:, 3, :], 'kout')
            sp.wait_ge(S['u_stored'], 16 * T)
            sp.wait_ge(S['proj_ps'], T)
            ld(uc[0:NCH, :, :], u_dram.rearrange("(c s) n -> c s n", s=L), 'uc_ld')
            sp.wait_ge(S['qk_ready'], 5)
            ld(A['attn_k_sample'][0, 0].rearrange("s h d -> s (h d)"), qk[0:DEC, 512:640], 'kout')
            ld(A['attn_v_sample'][0, 0].rearrange("s h d -> s (h d)"), vt[0:DEC, 5, :], 'kout')
            sp.wait_ge(S['k_sb'], 2)
            sp.wait_ge(S['ssm_made'], 2)
            for s in range(L):
                for r in range(4):
                    ld(M[s * SG:s * SG + SG, 8 * r:8 * r + 8, s * SG:P],
                       Kt[32 * r:32 * r + 16, :, :, 0:P - s * SG].rearrange("p g a n -> p (g a) n"), 'm_ready')
            sp.wait_ge(S['b_ps'], 6)
            ld(w_out_a[:, :, :], A['w_out'][0, 0:512, :].rearrange("(p k) n -> p k n", k=4), 'ld_wout')
            sp.wait_ge(S['cleared'], 1)
            for h in range(4):
                cols = slice(256 * h, 256 * h + 256)
                ld(slots_in[0:24 * P, cols].rearrange("(b p) n -> p b n", p=P),
                   zero[:, :].unsqueeze(1).to_broadcast([P, 24, 256]), 'zero_done')
                ld(slots_in[24 * P:NBLK * CAP, cols], zero[0:CAP, :], 'zero_done')
                ld(slots_out[33 * CAP:NBLK * CAP, cols].rearrange("(b p) n -> p b n", p=P),
                   zero[:, :].unsqueeze(1).to_broadcast([P, 8, 256]), 'zero_done')
            sp.wait_ge(S['y_ps'], 6)
            ld(w_ck[:, :, :], A['w_ck'][0].rearrange("(p k) n -> p k n", k=8), 'ld_wc')
            ld(memx[:, :, :], A['mem_prompt'][0].rearrange("(a p) n -> p a n", p=P), 'ld_mem')
            ld(cmk[:, :, :], A['cache_mem_k'][0, 0].rearrange("(a p) h d -> p a (h d)", p=P), 'ld_mem')
            ld(gck, A['ck_norm'][0].partition_broadcast(P), 'ld_mem')
            sp.wait_ge(S['z_ps'], 6)
            ld(w_out_s[:, :, :], A['w_out'][0, 512:1024, :].rearrange("(k p) n -> p k n", p=P), 'ld_wout2')
            sp.wait_ge(S['at_ps'], T)
            ld(wr[:, :, 0:4], A['w_router_group'][0].rearrange("(p k) n -> p k n", k=8), 'ld_wr')
            ld(wr[:, :, 4:36], A['w_router_expert'][0].rearrange("(p k) n -> p k n", k=8), 'ld_wr')
            ld(brt[:, 0:4], A['b_router_group'][0].partition_broadcast(P), 'ld_wr')
            ld(brt[:, 4:36], A['b_router_expert'][0].partition_broadcast(P), 'ld_wr')
            sp.wait_ge(S['kout'], 64)
            ld(mv[:, 2:4, :], A['cache_mem_v'][0, 0].rearrange("(a p) h d -> p a (h d)", p=P), 'ld_mem')
            sp.wait_ge(S['my_ps'], 8)
            sp.wait_ge(S['fin_out'], 64)
            ld(w_cv[:, :, :], A['w_cv'][0].rearrange("(p k) n -> p k n", k=8), 'ld_wcv')
            ld(w_cq[:, :, :], A['w_cq'][0].rearrange("(p k) n -> p k n", k=8), 'ld_wcq')
            ld(w_co[:, :, :], A['w_co'][0].rearrange("(k p) n -> p k n", p=P), 'ld_wco')
            for a in range(2):
                sp.wait_ge(S['mkn'], a + 1)
                ld(A['mem_k_prompt'][0, 0, a * P:a * P + P].rearrange("s h d -> s (h d)"), mkt[a], 'mem_out')
            for a in range(2):
                sp.wait_ge(S['mv_sb'], a + 1)
                ld(A['mem_v_prompt'][0, 0, a * P:a * P + P].rearrange("s h d -> s (h d)"), mv[:, a, :], 'mem_out')
            gate = A['w_e_gate'][0].rearrange("e (p k) n -> e p (k n)", p=P)
            up = A['w_e_up'][0].rearrange("e (p k) n -> e p (k n)", p=P)
            down = A['w_e_down'][0].rearrange("e (k p) n -> e p k n", p=P)

            def load_gate_up(j, e):
                s = slot[PHYS[j]]
                sp.dma_start(s[:, 0:4096], gate[e]).then_inc(S[f'lg{j}'], 16)
                sp.dma_start(s[:, 4096:8192], up[e]).then_inc(S[f'lg{j}'], 16)

            def load_down(j, e):
                s = slot[PHYS[j]]
                sp.dma_start(s[:, 8192:12288].rearrange("p (k n) -> p k n", k=4), down[e]).then_inc(S[f'ldn{j}'], 16)

            sp.wait_ge(S['mk_ps'], 2)
            sp.wait_ge(S['wo_ps'], 2 * T)
            load_gate_up(0, 0)
            load_down(0, 0)
            sp.wait_ge(S['mem_out'], 64)
            sp.wait_ge(S['mkT_ps'], 4)
            sp.wait_ge(S['mv_ps'], 2)
            sp.wait_ge(S['ssc'], T)
            load_gate_up(1, 1)
            load_down(1, 1)
            sp.wait_ge(S['cq_ps'], T)
            load_gate_up(2, 2)
            sp.wait_ge(S['cw_ps'], T)
            load_down(2, 2)

            def reload(j, e, used):
                s = slot[PHYS[j]]
                sp.wait_ge(S['gu_used'], used)
                sp.dma_start(s[:, 0:4096], gate[bass.ds(e, 1)].rearrange("a p m -> p (a m)")).then_inc(S[f'lg{j}'], 16)
                sp.dma_start(s[:, 4096:8192], up[bass.ds(e, 1)].rearrange("a p m -> p (a m)")).then_inc(S[f'lg{j}'], 16)
                sp.wait_ge(S['dn_used'], used)
                sp.dma_start(s[:, 8192:12288].rearrange("p (k n) -> p k n", k=4),
                             down[bass.ds(e, 1)].rearrange("a p k n -> p (a k) n")).then_inc(S[f'ldn{j}'], 16)

            with sp.Fori(1, 10) as it:
                for j in range(3):
                    reload(j, it * 3 + j, it * 3 + (j - 2))
            reload(0, 30, 28)
            reload(1, 31, 29)
            sp.wait_ge(S['slots_ready'], 2)
            e32 = sp.value_load(ovf[0:1, 0:1], min_val=0, max_val=NEXP - 1)
            reload(2, e32, 30)
            novf = sp.value_load(ovf[0:1, N_OVF:N_OVF + 1], min_val=0, max_val=N_OVF)
            with sp.If(novf > 1):
                with sp.Fori(0, N_OVF - 1) as k:
                    with sp.If(novf > k + 1):
                        e = sp.value_load(ovf[0:1, bass.ds(k + 1, 1)], min_val=0, max_val=NEXP - 1)
                        sp.wait_ge(S['v_go'], k + 1)
                        s = slot[PHYS[0]]
                        sp.dma_start(s[:, 0:4096], gate[bass.ds(e, 1)].rearrange("a p m -> p (a m)")).then_inc(S['v_w'], 16)
                        sp.dma_start(s[:, 4096:8192], up[bass.ds(e, 1)].rearrange("a p m -> p (a m)")).then_inc(S['v_w'], 16)
                        sp.dma_start(s[:, 8192:12288].rearrange("p (k n) -> p k n", k=4),
                                     down[bass.ds(e, 1)].rearrange("a p k n -> p (a k) n")).then_inc(S['v_w'], 16)
                        sp.nop()
                    sp.nop()
                sp.nop()
            sp.wait_ge(S['kout'], 64)
            sp.wait_ge(S['mem_out'], 64)
            sp.wait_ge(S['fin_out'], 64)
            sp.wait_ge(S['out_st'], 16 * T)

        @block.gpsimd
        def _(pool):
            def ld(dst, src, s):
                pool.dma_start(dst, src).then_inc(S[s], 16)

            ld(rope[:, :, :, :].rearrange("p a b c -> p (a b c)"), A['c_rope'], 'ld_const')
            ld(gqk[:, 0, :], A['q_norm'][0].partition_broadcast(P), 'ld_const')
            ld(gqk[:, 1, :], A['k_norm'][0].partition_broadcast(P), 'ld_const')
            ld(maskf[:, :], A['c_mask'], 'ld_const')
            ld(trif[:, :], A['c_tri'], 'ld_const')
            ld(sinkr[:, 0, :], A['attn_sink'][0].partition_broadcast(P), 'ld_const')
            ld(gcol[:, 8:16], A['norm_cross'][0].rearrange("(p k) -> p k", p=P), 'ld_const')
            ld(gcol[:, 16:24], A['norm_mem'][0].rearrange("(p k) -> p k", p=P), 'ld_const')
            ld(gcol[:, 24:28], A['norm_attn_out'][0].rearrange("(p k) -> p k", p=P), 'ld_const')
            ld(gcol[:, 32:33], A['cq_norm'][0].rearrange("(p k) -> p k", k=1), 'ld_const')
            ld(gcol[:, 34:42], A['norm_ffn'][0].rearrange("(p k) -> p k", p=P), 'ld_const')
            ld(vt[:, 4, :], A['cache_attn_v'][0, 0].rearrange("s h d -> s (h d)"), 'ld_const')

            step = [0]

            def link(ins):
                step[0] += 1
                ins.then_inc(S['pool_step'], 1)
                pool.wait_ge(S['pool_step'], step[0])

            def tt(o, a, b, op):
                link(pool.tensor_tensor(o, a, b, op))

            pool.wait_ge(S['pow_ready'], 1)
            for half in range(2):
                gs = slice(16 * half, 16 * half + 16)
                shp = [P, 16, 9, SG]
                pw = lambda i: powS[:, i, gs].unsqueeze(3).to_broadcast(shp)
                cs = lambda i: CS[:, i, gs].unsqueeze(2).to_broadcast(shp)
                V4 = V[:, gs].rearrange("p a (n m) -> p a n m", m=SG)
                t4 = pooltmp.rearrange("p (a n m) -> p a n m", a=16, n=9)
                tt(t4, pw(1), cs(1), ALU.mult)
                tt(V4, pw(0), cs(0), ALU.mult)
                tt(V4, V4, t4, ALU.add)
            pool.nop().then_inc(S['ssm_made'], 1)

            pool.wait_ge(S['wb_ready'], 1)
            pool.wait_ge(S['cst'], 1)
            pool.memset(M.rearrange("p a b -> p (a b)"), 0.0).then_inc(S['ssm_made'], 1)

            pool.wait_ge(S['wt_ps'], 8)
            link(pool.memset(GLU.rearrange("p a b -> p (a b)"), 0.0))
            for s in range(L):
                ld(GLU[s * SG:s * SG + SG, :, s * SG:s * SG + SG],
                   A['ssm_w_glu'][0].rearrange("g p q -> p g q"), 'ld_glu')
            pool.wait_ge(S['fin_sb'], 1)
            for i, n in enumerate(('ssm_re_prompt', 'ssm_im_prompt', 'ssm_re_sample', 'ssm_im_sample')):
                ld(A[n][0, 0].rearrange("(a b) n -> a (b n)", b=2), finrow[0:16, 128 * i:128 * i + 128], 'fin_out')

            pool.wait_ge(S['ld_wr'], 96)
            for t in range(T):
                r = ROWS[t]
                pool.wait_ge(S['h3a'], t + 1)
                link(pool.tensor_tensor(h3[t][0:r, :], h3[t][0:r, :], gffn[0:r, :], ALU.mult))
            pool.wait_ge(S['zero_done'], 192)
            pool.wait_ge(S['slots_ready'], 1)
            for t in range(T):
                r = ROWS[t]
                for c in range(2):
                    pool.indirect_dma_start(
                        out=slots_in, out_offset=bass.IndirectOffsetOnAxis(ap=idx[0:r, 5 * c + t:5 * c + t + 1], axis=0),
                        in_=h3[t][0:r, :], in_offset=None).then_inc(S[f'sc_done{t % 2}'], 16)
            pool.wait_ge(S['sc_done0'], 96)
            pool.wait_ge(S['sc_done1'], 64)

            def load_x(b, j, waited):
                if waited is not None:
                    pool.wait_ge(S['xgt_ps'], waited)
                    pool.nop()
                pool.dma_start(xg[j][0:CAP, :], slots_in[bass.ds(b * CAP, CAP), :]).then_inc(S[f'xg_ld{j}'], 16)

            def store_y(b, j, count):
                pool.wait_ge(S['y_ready'], count)
                pool.nop()
                for h in range(2):
                    pool.dma_start(slots_out[bass.ds(b * CAP, CAP), h * 512:h * 512 + 512],
                                   yb[j][64 * h:64 * h + 64, :]).then_inc(S[f'y_out{j}'], 16)

            load_x(0, 0, None)
            load_x(1, 1, None)
            with pool.Fori(0, 15) as it:
                for j in range(2):
                    load_x(it * 2 + (j + 2), j, it * 2 + (j + 1))
                    store_y(it * 2 + j, j, it * 2 + (j + 1))
            load_x(32, 0, 31)
            store_y(30, 0, 31)
            store_y(31, 1, 32)
            store_y(32, 0, 33)
            pool.wait_ge(S['slots_ready'], 2)
            novf = pool.value_load(ovf[0:1, N_OVF:N_OVF + 1], min_val=0, max_val=N_OVF)
            pool.wait_ge(S['y_out0'], 32 * 17)
            pool.wait_ge(S['y_out1'], 32 * 16)
            with pool.If(novf > 1):
                with pool.Fori(0, N_OVF - 1) as k:
                    with pool.If(novf > k + 1):
                        pool.wait_ge(S['v_go'], k + 1)
                        pool.nop()
                        pool.dma_start(xg[0][0:CAP, :], slots_in[bass.ds((k + 33) * CAP, CAP), :]).then_inc(S['xg_ld0'], 16)
                        pool.wait_ge(S['y_more'], k * 32 + 32)
                        pool.nop()
                    pool.nop()
                pool.nop()
            for t in range(T):
                r = ROWS[t]
                for c in range(2):
                    pool.indirect_dma_start(
                        out=yg[t][c][0:r, :], out_offset=None, in_=slots_out,
                        in_offset=bass.IndirectOffsetOnAxis(ap=idx[0:r, 5 * c + t:5 * c + t + 1], axis=0)
                    ).then_inc(S[f'gath{t}'], 16)

        @block.tensor
        def _(pe):
            def tr(out, in_, n, s=None):
                i = pe.transpose(out, in_, ident[0:n, 0:n])
                if s:
                    i.then_inc(S[s], 1)
                return i

            def small():
                pe.wait_ge(S['sm'], 1)
                for i in range(5):
                    tr(bank[7][:, 16 * i:16 * i + 16], smrow[0:16, 128 * i:128 * i + 128], 16)
                tr(bank[7][:, 128:160], smrow[0:32, 768:896], 32)
                tr(bank[7][:, 160:192], smrow[0:32, 896:1024], 32)
                tr(bank[7][:, 192:196], smrow[0:4, 640:768], 4, 'sm_ps')

            def c_transposes(a):
                pe.wait_ge(S['ld_c'], 64)
                if a == 0:
                    pe.wait_ge(S['sm'], 2)
                else:
                    pe.wait_ge(S['c_sb'], 1)
                for i in range(4):
                    m = tr(bank[7][:, P * i:P * i + P], Craw[:, a, i, :, :].rearrange("p d n -> p (d n)"), P)
                m.then_inc(S['c_ps'], 1)

            def x_transposes(t):
                r = ROWS[t]
                pe.wait_ge(S[f'ld_x{t}'], 16)
                if t == 0:
                    pe.wait_ge(S['ld_ident'], 16)
                xv = x[:, t, :].rearrange("p (q k) -> p k q", k=8)
                for h in range(2):
                    if t:
                        pe.wait_ge(S['xt_sb'], 2 * (t - 1) + h + 1)
                    for k in range(4):
                        m = tr(bank[h][:, r * k:r * k + r], xv[0:r, 4 * h + k, :], r)
                    m.then_inc(S['xt_ps'], 1)

            def project(t):
                r = ROWS[t]
                pe.wait_ge(S['xt_sb'], 2 * t + 2)
                if t:
                    pe.wait_ge(S['proj_sb'], t)
                u_rows = UROWS[t]
                for k in range(8):
                    if t == 0 and k % 4 == 0:
                        pe.wait_ge(S[f'ld_win{k // 4}'], 32)
                    lhs = xT[:, k, TOK0[t]:TOK0[t] + r]
                    pe.matmul(bank[3][0:r, 0:256], lhs, w_in[:, k, 512:768], start=k == 0, stop=k == 7)
                    pe.matmul(bank[2][0:r, :], lhs, w_in[:, k, 0:512], start=k == 0, stop=k == 7)
                    m = pe.matmul(bank[4][u_rows, :], lhs, w_in[:, k, 768:1280], start=k == 0, stop=k == 7)
                    if t == 4 and 4 <= k < 7:
                        w_transposes(k - 4)
                m.then_inc(S['proj_ps'], 1)
                if t == 4:
                    w_transposes(3)

            def qk_transposes(n):
                if n < 5:
                    r = ROWS[n]
                    pe.wait_ge(S['qk_ready'], n + 1)
                    if n:
                        pe.wait_ge(S['qkt_sb'], n)
                    for i in range(4):
                        tr(bank[5][:, P * i:P * i + r], qk[0:r, P * i:P * i + P], r)
                else:
                    r = P
                    pe.wait_ge(S['ld_cache'], 32)
                    pe.wait_ge(S['qkt_sb'], n)
                for i in range(2):
                    m = tr(bank[6 if n < 5 else 5][:, P * i:P * i + r],
                           kdup[0:r, 2 * i:2 * i + 2, :].rearrange("p d n -> p (d n)"), r)
                m.then_inc(S['qk_ps'], 1)

            def w_transposes(u):
                if u == 0:
                    pe.wait_ge(S['wb_ready'], 1)
                    pe.wait_ge(S['c_sb'], 2)
                else:
                    pe.wait_ge(S['wt_sb'], u)
                for i in range(4):
                    a, pr = divmod(4 * u + i, NPAIR)
                    m = tr(bank[7][:, P * i:P * i + P], WB[:, a, pr, :], P)
                m.then_inc(S['wt_ps'], 1)

            def k_matmuls():
                pe.wait_ge(S['ssm_made'], 1)
                pe.wait_ge(S['bb_ready'], 1)
                for g2 in range(2):
                    if g2 == 0:
                        pe.wait_ge(S['wt_sb'], 8)
                    else:
                        pe.wait_ge(S['k_sb'], 1)
                    for pr in range(NPAIR):
                        a, r = divmod(pr, 4)
                        m = pe.matmul(bank[7][32 * r:32 * r + 16, P * a:P * a + P], BbS[:, 2 * pr + g2, :],
                                      V[:, 2 * pr + g2, 0:P], start=True, stop=True)
                    m.then_inc(S['k_ps'], 1)

            def ssm_bank(u):
                return bank[6 + u % 2]

            def u_transposes():
                pe.wait_ge(S['ucg'], 2)
                pe.wait_ge(S['qkt_sb'], 5)
                pe.wait_ge(S['k_sb'], 2)
                for u, (lo, hi) in enumerate(UNITS):
                    if u >= 2:
                        pe.wait_ge(S['u_sb'], u - 1)
                    for o in range(lo, hi):
                        g = 2 * (o % 16) + o // 16
                        m = tr(ssm_bank(u)[:, (o - lo) * NCH:(o - lo + 1) * NCH],
                               ucg[0:NCH, g, :], NCH)
                    m.then_inc(S['u_ps'], 1)

            def b_matmuls():
                pe.wait_ge(S['u_sb'], 6)
                for u, (lo, hi) in enumerate(UNITS):
                    if u >= 2:
                        pe.wait_ge(S['b_sb'], u - 1)
                    for o in range(lo, hi):
                        a, pr = divmod(o, NPAIR)
                        for g2 in range(2):
                            og = g2 * 16 + pr
                            m = pe.matmul(ssm_bank(u)[64 * g2:64 * g2 + 64, (o - lo) * NCH:(o - lo + 1) * NCH],
                                          Wt[:, a, pr, 64 * g2:64 * g2 + 64], U[:, og * NCH:og * NCH + NCH],
                                          start=True, stop=True)
                    m.then_inc(S['b_ps'], 1)

            def y_matmuls():
                pe.wait_ge(S['b_sb'], 6)
                pe.wait_ge(S['h_ready'], 1)
                pe.wait_ge(S['m_ready'], 16 * 32)
                for u, (lo, hi) in enumerate(UNITS):
                    if u >= 2:
                        pe.wait_ge(S['y_sb'], u - 1)
                    for o in range(lo, hi):
                        g2, pr = divmod(o, NPAIR)
                        a, r = divmod(pr, 4)
                        out = ssm_bank(u)[:, (o - lo) * NCH:(o - lo + 1) * NCH]
                        pe.matmul(out, M[:, 8 * r + 4 * g2 + a, :], U[:, o * NCH:o * NCH + NCH], start=True, stop=False)
                        m = pe.matmul(out, V[:, 2 * pr + g2, 16:144], H[:, o, 0:NCH], start=False, stop=True)
                    m.then_inc(S['y_ps'], 1)

            def fin_transposes():
                pe.wait_ge(S['h_ready'], 1)
                pe.wait_ge(S['y_sb'], 6)
                for i in range(4):
                    m = tr(bank[6][0:16, P * i:P * i + P], fin[:, i, :], P)
                m.then_inc(S['fin_ps'], 1)

            def z_matmuls():
                pe.wait_ge(S['ssm_act'], 1)
                pe.wait_ge(S['ld_glu'], 16 * L)
                pe.wait_ge(S['fin_sb'], 1)
                for u, (lo, hi) in enumerate(UNITS):
                    if u >= 2:
                        pe.wait_ge(S['z_sb'], u - 1)
                    for o in range(lo, hi):
                        g = 2 * (o % 16) + o // 16
                        m = pe.matmul(ssm_bank(u)[:, (o - lo) * NCH:(o - lo + 1) * NCH], GLU[:, g, :],
                                      Y[:, o * NCH:o * NCH + NCH], start=True, stop=True)
                    m.then_inc(S['z_ps'], 1)

            def yt_transposes():
                pe.wait_ge(S['glu_done'], 1)
                for u in range(8):
                    if u >= 2:
                        pe.wait_ge(S['yt_sb'], u - 1)
                    for i in range(4):
                        g = 4 * u + i
                        o = (g % 2) * 16 + g // 2
                        m = tr(ssm_bank(u)[0:NCH, P * i:P * i + P], Y[:, o * NCH:o * NCH + NCH], P)
                    m.then_inc(S['yt_ps'], 1)

            def my_transposes():
                for u in range(8):
                    k, th = divmod(u, 2)
                    pe.wait_ge(S['yn'], 4 * th + 4 if k == 0 else 8)
                    if u < 2:
                        pe.wait_ge(S['yt_sb'], 8)
                    else:
                        pe.wait_ge(S['my_sb'], u - 1)
                    for i in range(4):
                        m = tr(ssm_bank(u)[:, NCH * i:NCH * i + NCH], yc[0:NCH, 4 * th + i, P * k:P * k + P], NCH)
                    m.then_inc(S['my_ps'], 1)

            def scores(i):
                r = ROWS[i]
                if i == 0:
                    pe.wait_ge(S['qkt_sb'], 4)
                    pe.wait_ge(S['cst'], 1)
                if i == 4:
                    pe.wait_ge(S['qkt_sb'], 6)
                    pe.wait_ge(S['ld_const'], 16 * 12)
                k0, w = (0, P) if i == 0 else (512, 192) if i == 4 else ((i - 1) * P, 2 * P)
                for b in range(4):
                    par, kv = divmod(b, 2)
                    rows = slice(64 * par, 64 * par + 64)
                    if i:
                        pe.wait_ge(S['pt_sb'], 4 * (i - 1) + b + 1)
                    if i < 4:
                        for s in range(2):
                            pe.matmul(bank[b][:, 256 * s:256 * s + w], maskb[rows, 0:P],
                                      maskb[rows, P + 256 - w:P + 256], start=s == 0, stop=False, skip_group_check=True)
                    for s in range(2):
                        m = pe.matmul(bank[b][0:r, 256 * s:256 * s + w], qT[rows, 2 * kv + s, TOK0[i]:TOK0[i] + r],
                                      kT[rows, kv, k0:k0 + w], start=i == 4 and s == 0, stop=s == 1,
                                      skip_group_check=True)
                m.then_inc(S['s_ps'], 1)

            def att_out(i):
                r = ROWS[i]
                nk = 1 if i == 0 else 2
                kw = [P] if i == 0 else [P, P] if i < 4 else [P, 64]
                pe.wait_ge(S['expd'], 9 * i + 9)
                for b in range(4):
                    for s in range(2):
                        for c in range(nk):
                            m = tr(bank[b][0:kw[c], (2 * s + c) * P:(2 * s + c) * P + r],
                                   Prob[0:r, 2 * b + s, c * P:c * P + kw[c]], r)
                    m.then_inc(S['p_ps'], 1)
                for b in range(4):
                    pe.wait_ge(S['pt_sb'], 4 * i + b + 1)
                    if b == 0 and i:
                        pe.wait_ge(S['x1'], i)
                    for s in range(2):
                        o = 2 * b + s
                        kv = b % 2
                        for c in range(nk):
                            vi = 4 + c if i == 4 else (i - (nk - 1) + c)
                            m = pe.matmul(bank[4][0:r, 64 * o:64 * o + 64], PT[0:kw[c], 2 * o + c, 0:r],
                                          vt[0:kw[c], vi, 64 * kv:64 * kv + 64],
                                          start=o == 0 and c == 0, stop=c == nk - 1, skip_group_check=True)
                m.then_inc(S['o_ps'], 1)

            def att_transposes(i):
                r = ROWS[i]
                pe.wait_ge(S['a_norm'], i + 1)
                av = atile.rearrange("p (q k) -> p k q", k=4)
                for k in range(4):
                    m = tr(bank[5][:, r * k:r * k + r], av[0:r, k, :], r)
                m.then_inc(S['at_ps'], 1)

            def out_attention(t):
                r = ROWS[t]
                if t == 0:
                    pe.wait_ge(S['ld_wout'], 16)
                pe.wait_ge(S['at_sb'], t + 1)
                for k in range(4):
                    for h in range(2):
                        m = pe.matmul(bank[4 + h][half_rows(t, h), :], mixT[:, k, TOK0[t]:TOK0[t] + r],
                                      w_out_a[:, k, 512 * h:512 * h + 512], start=k == 0, stop=k == 3)
                m.then_inc(S['wo_ps'], 1)

            def out_ssm(t):
                r = ROWS[t]
                if t == 0:
                    pe.wait_ge(S['ld_wout2'], 16)
                    pe.wait_ge(S['my_sb'], 8)
                    pe.wait_ge(S['mt_sb'], 4)
                if t >= 2:
                    pe.wait_ge(S['x1'], T + t - 1)
                for k in range(4):
                    for h in range(2):
                        m = pe.matmul(bank[2 * (t % 2) + h][half_rows(t, h), :], mixT[:, 4 + k, TOK0[t]:TOK0[t] + r],
                                      w_out_s[:, k, 512 * h:512 * h + 512], start=k == 0, stop=k == 3)
                m.then_inc(S['wo_ps'], 1)

            def mem_transposes(a):
                if a == 0:
                    pe.wait_ge(S['ld_mem'], 64)
                    pe.wait_ge(S['pt_sb'], 20)
                mxv = memx[:, a, :].rearrange("p (q k) -> p k q", k=8)
                for h in range(2):
                    for k in range(4):
                        m = tr(bank[2 * a + h][:, P * k:P * k + P], mxv[:, 4 * h + k, :], P)
                    m.then_inc(S['mt_ps'], 1)

            def mem_k(a):
                pe.wait_ge(S['mt_sb'], 2 * a + 2)
                pe.wait_ge(S['ld_wc'], 16)
                pe.wait_ge(S['x1'], T)
                for k in range(8):
                    m = pe.matmul(bank[4 + a][:, :], memT[:, k, P * a:P * a + P], w_ck[:, k, :], start=k == 0, stop=k == 7)
                m.then_inc(S['mk_ps'], 1)

            def mem_v(a):
                pe.wait_ge(S['ld_wcv'], 16)
                for k in range(8):
                    m = pe.matmul(bank[6 + a][:, :], memT[:, k, P * a:P * a + P], w_cv[:, k, :], start=k == 0, stop=k == 7)
                m.then_inc(S['mv_ps'], 1)

            def mk_transposes(n):
                if n < 2:
                    pe.wait_ge(S['mkn'], n + 1)
                    src = mkt[n]
                else:
                    pe.wait_ge(S['mkT_sb'], n - 1)
                    src = cmk[:, n - 2, :]
                for h in range(CAH):
                    m = tr(bank[4 + n % 2][:, P * h:P * h + P], src[:, P * h:P * h + P], P)
                m.then_inc(S['mkT_ps'], 1)

            def cross_q(t):
                r = ROWS[t]
                if t == 0:
                    pe.wait_ge(S['x1'], 2 * T)
                elif t > 1:
                    pe.wait_ge(S['x2'], t - 1)
                xv = x[:, t, :].rearrange("p (q k) -> p k q", k=8)
                for h in range(2):
                    for k in range(4):
                        m = tr(bank[h][:, r * k:r * k + r], xv[0:r, 4 * h + k, :], r)
                    m.then_inc(S['xt_ps'], 1)
                pe.wait_ge(S['ld_wcq'], 16)
                for k in range(8):
                    if k % 4 == 0:
                        pe.wait_ge(S['xt_sb'], 2 * (T + t) + k // 4 + 1)
                    if t < 4:
                        m = pe.matmul(bank[2][0:r, :], x1T[:, k, 0:r], w_cq[:, k, :], start=k == 0, stop=k == 7)
                    else:
                        for h in range(2):
                            m = pe.matmul(bank[2][half_rows(t, h), 0:256], x1T[:, k, 0:r], w_cq[:, k, 256 * h:256 * h + 256],
                                          start=k == 0, stop=k == 7)
                m.then_inc(S['cq_ps'], 1)

            def cross_scores(t):
                r = ROWS[t]
                pe.wait_ge(S['cqn'], t + 1)
                if t == 0:
                    pe.wait_ge(S['x1'], 2 * T)
                    pe.wait_ge(S['mkT_sb'], 4)
                for h in range(CAH):
                    m = tr(bank[3][:, P * h:P * h + r], qc[0:r, P * h:P * h + P], r)
                m.then_inc(S['cqT_ps'], 1)
                pe.wait_ge(S['cqT_sb'], t + 1)
                k0 = 256 if t == 4 else 0
                for h in range(CAH):
                    m = pe.matmul(bank[4 + h // 2][0:r, 256 * (h % 2):256 * (h % 2) + 256], qcT[:, h, 0:r],
                                  mkT[:, h, k0:k0 + 256], start=True, stop=True)
                m.then_inc(S['cs_ps'], 1)

            def cross_out(t):
                r = ROWS[t]
                if t == 0:
                    pe.wait_ge(S['mv_sb'], 2)
                pe.wait_ge(S['cpn'], t + 1)
                for h in range(CAH):
                    for c in range(2):
                        m = tr(bank[6 + h // 2][:, (2 * (h % 2) + c) * P:(2 * (h % 2) + c) * P + r],
                               cP[0:r, h, P * c:P * c + P], r)
                    if h % 2:
                        m.then_inc(S['cp_ps'], 1)
                v0 = 2 if t == 4 else 0
                for h in range(CAH):
                    if h % 2 == 0:
                        pe.wait_ge(S['cpt_sb'], 2 * t + h // 2 + 1)
                    for c in range(2):
                        m = pe.matmul(bank[3][:, P * h:P * h + r], mv[:, v0 + c, P * h:P * h + P], cPT[:, 2 * h + c, 0:r],
                                      start=c == 0, stop=c == 1)
                m.then_inc(S['co_ps'], 1)
                pe.wait_ge(S['co_sb'], t + 1)
                pe.wait_ge(S['ld_wco'], 16)
                for k in range(4):
                    for h in range(2):
                        m = pe.matmul(bank[h][half_rows(t, h), :], oT[:, k, 0:r], w_co[:, k, 512 * h:512 * h + 512],
                                      start=k == 0, stop=k == 3)
                m.then_inc(S['cw_ps'], 1)

            def router_transposes(t):
                r = ROWS[t]
                pe.wait_ge(S['x2'], T)
                if t >= 2:
                    pe.wait_ge(S['h3T_sb'], 2 * (t - 1))
                xv = x[:, t, :].rearrange("p (q k) -> p k q", k=8)
                for h in range(2):
                    for k in range(4):
                        m = tr(bank[2 * (t % 2) + h][:, r * k:r * k + r], xv[0:r, 4 * h + k, :], r)
                    m.then_inc(S['h3T_ps'], 1)

            def router_logits(t):
                r = ROWS[t]
                pe.wait_ge(S['ld_wr'], 96)
                for k in range(8):
                    if k % 4 == 0:
                        pe.wait_ge(S['h3T_sb'], 2 * t + k // 4 + 1)
                    m = pe.matmul(bank[4][0:r, 36 * t:36 * t + 36], x2T[:, k, 0:r], wr[:, k, :], start=k == 0, stop=k == 7,
                                  skip_group_check=True)
                m.then_inc(S['lg_ps'], 1)

            def counts():
                pe.wait_ge(S['oh_ready'], 1)
                """Of each expert: how many tokens of a tile stand before a token, and how many there are."""
                pe.matmul(bank[5][:, 0:160], trib[:, 0:P], hotb, start=True, stop=True)
                pe.matmul(bank[6][:, 0:160], trib[:, P:2 * P], hotb, start=True, stop=True).then_inc(S['cnt_ps'], 1)

            x_transposes(0)
            project(0)
            small()
            x_transposes(1)
            c_transposes(0)
            c_transposes(1)
            x_transposes(2)
            project(1)
            qk_transposes(0)
            x_transposes(3)
            project(2)
            qk_transposes(1)
            x_transposes(4)
            project(3)
            qk_transposes(2)
            project(4)
            for u in range(4, 8):
                w_transposes(u)
            qk_transposes(3)
            k_matmuls()
            scores(0)
            qk_transposes(4)
            u_transposes()
            qk_transposes(5)
            b_matmuls()
            att_out(0)
            scores(1)
            att_transposes(0)
            out_attention(0)
            att_out(1)
            scores(2)
            att_transposes(1)
            out_attention(1)
            y_matmuls()
            att_out(2)
            scores(3)
            att_transposes(2)
            fin_transposes()
            out_attention(2)
            z_matmuls()
            att_out(3)
            scores(4)
            att_transposes(3)
            out_attention(3)
            yt_transposes()
            att_out(4)
            att_transposes(4)
            out_attention(4)
            my_transposes()
            mem_transposes(0)
            mem_transposes(1)
            mem_k(0)
            mem_k(1)
            for t in range(3):
                out_ssm(t)
            mk_transposes(0)
            mk_transposes(1)
            out_ssm(3)
            out_ssm(4)
            mem_v(0)
            mem_v(1)
            mk_transposes(2)
            mk_transposes(3)
            cross_q(0)
            cross_scores(0)
            for t in range(T):
                if t < 4:
                    cross_q(t + 1)
                cross_out(t)
                if t < 4:
                    cross_scores(t + 1)
            router_transposes(0)
            for t in range(T):
                if t < 4:
                    router_transposes(t + 1)
                router_logits(t)
            counts()

            def half_cols(w, h):
                return w[:, 0:8192].rearrange("p (g k n) -> p k g n", g=2, k=8)[:, :, :, 256 * h:256 * h + 256]

            def x_block(j, waits):
                for s, v in waits:
                    pe.wait_ge(S[s], v)
                xv = xg[j][0:CAP, :].rearrange("p (q k) -> p k q", k=8)
                pe.matmul(bank[j][:, 0:CAP], xv[:, 0, :], ident[0:CAP, 0:CAP], start=True, stop=True)
                for k in range(1, 8):
                    m = tr(bank[j][:, CAP * k:CAP * k + CAP], xv[:, k, :], CAP)
                return m

            def gate_up(w, j):
                for k in range(8):
                    for h in range(2):
                        m = pe.matmul(bank[2 + j][64 * h:64 * h + 64, :], xgT[j][:, k, :], half_cols(w, h)[:, k, :, :],
                                      start=k == 0, stop=k == 7, skip_group_check=True)
                return m

            def h_block():
                for i in range(2):
                    m = tr(bank[4][:, P * i:P * i + P], hact[:, P * i:P * i + P], P)
                return m

            def down_block(w, j):
                wd = w[:, 8192:12288].rearrange("p (k n) -> p k n", k=4)
                for n, (h, i) in enumerate(((0, 0), (0, 1), (1, 0), (1, 1))):
                    for c in range(2):
                        m = pe.matmul(bank[6 + j][64 * c:64 * c + 64, :], hT[:, i, 64 * h:64 * h + 64],
                                      wd[:, 2 * h + i, 512 * c:512 * c + 512], start=n == 0, stop=n == 3,
                                      skip_group_check=True)
                return m

            def expert(j, jj, b, n3, n2):
                w = slot[PHYS[j]]
                pe.wait_ge(S[f'xg_ld{jj}'], n2 * 16)
                pe.nop()
                x_block(jj, []).then_inc(S['xgt_ps'], 1)
                pe.wait_ge(S['xgt_sb'], b + 1)
                pe.wait_ge(S[f'lg{j}'], n3 * 32)
                gate_up(w, jj).then_inc(S['gu_used'], 1)
                pe.wait_ge(S['hact_ready'], b + 1)
                pe.nop()
                h_block().then_inc(S['ht_ps'], 1)
                pe.wait_ge(S['ht_sb'], b + 1)
                pe.wait_ge(S[f'ldn{j}'], n3 * 16)
                if not isinstance(b, int) or b >= 2:
                    pe.wait_ge(S['y_ready'], b - 1)
                down_block(w, jj).then_inc(S['dn_used'], 1)

            pe.wait_ge(S['h3T_sb'], 10)
            pe.wait_ge(S['slots_ready'], 2)
            for b in range(6):
                expert(b % 3, b % 2, b, b // 3 + 1, b // 2 + 1)
            with pe.Fori(1, 5) as it:
                for b in range(6):
                    expert(b % 3, b % 2, it * 6 + b, it * 2 + (b // 3 + 1), it * 3 + (b // 2 + 1))
            for b in range(30, 33):
                expert(b % 3, b % 2, b, b // 3 + 1, b // 2 + 1)
            novf = pe.value_load(ovf[0:1, N_OVF:N_OVF + 1], min_val=0, max_val=N_OVF)
            with pe.If(novf > 1):
                with pe.Fori(0, N_OVF - 1) as k:
                    with pe.If(novf > k + 1):
                        pe.wait_ge(S['xg_ld0'], k * 16 + 16 * 18)
                        pe.wait_ge(S['y_ready'], k + 33)
                        pe.nop()
                        x_block(0, []).then_inc(S['xgt_ps'], 1)
                        pe.wait_ge(S['xgt_sb'], k + 34)
                        pe.wait_ge(S['v_w'], k * 48 + 48)
                        gate_up(slot[PHYS[0]], 0).then_inc(S['gu_used'], 1)
                        pe.wait_ge(S['hact_ready'], k + 34)
                        pe.nop()
                        h_block().then_inc(S['ht_ps'], 1)
                        pe.wait_ge(S['ht_sb'], k + 34)
                        down_block(slot[PHYS[0]], 0).then_inc(S['dn_used'], 1)
                        pe.nop()
                    pe.nop()
                pe.nop()

        @block.scalar
        def _(act):
            def cp(out, in_, s, **kw):
                return act.activation(out, in_, ACT.Identity if kw else ACT.Copy, **kw).then_inc(S[s], 1)

            def ld(dst, src, s):
                act.dma_start(dst, src).then_inc(S[s], 16)

            ld(smrow[0:16, 0:128], A['ssm_lambda_re'][0].rearrange("(a b) n -> a (b n)", b=2), 'ld_ssm')
            ld(smrow[0:16, 128:256], A['ssm_lambda_im'][0].rearrange("(a b) n -> a (b n)", b=2), 'ld_ssm')
            ld(smrow[0:16, 384:512], A['state_ssm_re'][0, 0].rearrange("(a b) n -> a (b n)", b=2), 'ld_ssm')
            ld(smrow[0:16, 512:640], A['state_ssm_im'][0, 0].rearrange("(a b) n -> a (b n)", b=2), 'ld_ssm')
            ld(smrow[0:16, 1024:1026], A['ssm_log_dt'][0].rearrange("(a b) -> a b", b=2), 'ld_ssm')
            ld(smrow[0:32, 1026:1042], A['ssm_d'][0], 'ld_ssm')
            ld(smrow[0:32, 1042:1058], A['ssm_b_glu'][0], 'ld_ssm')
            ld(smrow[0:4, 640:768], A['norm_ssm_out'][0].rearrange("(a b) -> a b", b=P), 'ld_ssm')
            for a, n in ((0, 'ssm_c_re'), (1, 'ssm_c_im')):
                for d in range(2):
                    ld(Craw[:, a, :, d, :], A[n][0].rearrange("(a g) q n -> (g q) a n", a=4), 'ld_c')
            for a, n in ((0, 'ssm_b_re'), (1, 'ssm_b_im')):
                ld(Braw[:, a, :, :], A[n][0].rearrange("(a b) n p -> (b n) a p", b=2), 'ld_b')



            def squares(t):
                r = ROWS[t]
                act.wait_ge(S[f'ld_x{t}'], 16)
                if t:
                    act.wait_ge(S['ssx'], t)
                act.activation(x_sq[0:r, :], x[0:r, t, :], ACT.Square, accum_out=tiny[0:r, t:t + 1]).then_inc(S['ssx'], 1)



            act.wait_ge(S['cleared'], 1)
            for t in range(T):
                squares(t)

            def proj_evac_u(t):
                r = ROWS[t]
                act.wait_ge(S['proj_ps'], t + 1)
                act.wait_ge(S['rms'], 1)
                if t:
                    act.wait_ge(S['u_stored'], 16 * t)
                rt_ = tiny[0:r, 8 + t:9 + t]
                act.activation(usb[0:r, :], bank[4][UROWS[t], :], ACT.Identity, scale=rt_).then_inc(S['u_sent'], 1)
                act.activation(vt[0:r, VIDX[t], :], bank[3][0:r, 128:256], ACT.Identity, scale=rt_)

            def proj_evac_qk(t):
                r = ROWS[t]
                rt_ = tiny[0:r, 8 + t:9 + t]
                if t:
                    act.wait_ge(S['qk_ps'], t)
                if t == 4:
                    act.wait_ge(S['kout'], 32)
                act.activation(qk[0:r, 0:512], bank[2][0:r, :], ACT.Identity, scale=rt_)
                act.activation(qk[0:r, 512:640], bank[3][0:r, 0:128], ACT.Identity, scale=rt_).then_inc(S['proj_sb'], 1)

            def proj_evac(t):
                proj_evac_u(t)
                proj_evac_qk(t)

            def qkt_evac(n):
                act.wait_ge(S['qk_ps'], n + 1)
                if n < 5:
                    r = ROWS[n]
                    act.activation(qT[:, :, TOK0[n]:TOK0[n] + r],
                                   bank[5][:, :].rearrange("p (a b) -> p a b", a=4)[:, :, 0:r], ACT.Copy)
                    kc = KCOL[n]
                else:
                    r, kc = P, 512
                act.activation(kT[:, :, kc:kc + r],
                               bank[6 if n < 5 else 5][:, 0:256].rearrange("p (a b) -> p a b", a=2)[:, :, 0:r], ACT.Copy).then_inc(S['qkt_sb'], 1)

            def wt_evac(units):
                for u in units:
                    act.wait_ge(S['wt_ps'], u + 1)
                    a, pr = divmod(4 * u, NPAIR)
                    act.activation(Wt[:, a, pr:pr + 4, :].rearrange("p a b -> p (a b)"), bank[7][:, :], ACT.Copy
                                   ).then_inc(S['wt_sb'], 1)

            proj_evac(0)
            act.wait_ge(S['asked'], 1)
            act.activation(ssm_s[:, 8:10, :], ssm_s[:, 6:8, :], ACT.Sin).then_inc(S['answered'], 1)
            proj_evac(1)
            qkt_evac(0)
            proj_evac(2)
            qkt_evac(1)
            proj_evac(3)
            qkt_evac(2)
            wt_evac(range(3))
            proj_evac_u(4)
            wt_evac(range(3, 8))
            proj_evac_qk(4)
            qkt_evac(3)
            for g2 in range(2):
                act.wait_ge(S['k_ps'], g2 + 1)
                for r in range(4):
                    m = act.activation(Kt[32 * r:32 * r + 16, g2, :, :].rearrange("p a n -> p (a n)"),
                                       bank[7][32 * r:32 * r + 16, :], ACT.Copy)
                m.then_inc(S['k_sb'], 1)
            act.wait_ge(S['uc_ld'], 16)
            uview = uc[0:NCH].rearrange("p s (g b q) -> p b g s q", b=2, q=SG)
            gview = ucg[0:NCH].rearrange("p (g b) (s q) -> p b g s q", b=2, q=SG)
            act.activation(gview[:, 1], uview[:, 1], ACT.Copy).then_inc(S['ucg'], 1)
            qkt_evac(4)
            for d in range(2):
                act.dma_start(kdup.rearrange("p (a d) n -> p a d n", d=2)[:, :, d, :], A['cache_attn_k'][0, 0]
                              ).then_inc(S['ld_cache'], 16)

            def unit_evac(dst, ps, s):
                for u, (lo, hi) in enumerate(UNITS):
                    act.wait_ge(S[ps], u + 1)
                    act.activation(dst[:, lo * NCH:hi * NCH], bank[6 + u % 2][:, 0:(hi - lo) * NCH], ACT.Copy).then_inc(S[s], 1)

            def att_exp(i):
                r = ROWS[i]
                w = P if i == 0 else 192 if i == 4 else 256
                act.wait_ge(S['nmax'], i + 1)
                if i:
                    act.wait_ge(S['p_ps'], 4 * i)
                act.activation(tiny[0:r, 48:56], tiny[0:r, 40:48], ACT.Exp).then_inc(S['expd'], 1)
                for o in range(8):
                    act.activation(Prob[0:r, o, 0:w], bank[o // 2][0:r, 256 * (o % 2):256 * (o % 2) + w], ACT.Exp,
                                   bias=tiny[0:r, 32 + o:33 + o], accum_out=tiny[0:r, 56 + o:57 + o]).then_inc(S['expd'], 1)

            def pt_evac(i):
                r = ROWS[i]
                if i == 0:
                    act.wait_ge(S['m_ready'], 16 * 32)
                for b in range(4):
                    act.wait_ge(S['p_ps'], 4 * i + b + 1)
                    if b == 0 and i:
                        act.wait_ge(S['o_ps'], i)
                    ps = bank[b][:, :].rearrange("p (a b) -> p a b", a=4)
                    if i == 4:
                        act.activation(PT[:, 4 * b:4 * b + 4:2, 0:r], ps[:, 0:4:2, 0:r], ACT.Copy)
                        act.activation(PT[0:64, 4 * b + 1:4 * b + 4:2, 0:r], ps[0:64, 1:4:2, 0:r], ACT.Copy
                                       ).then_inc(S['pt_sb'], 1)
                    elif i == 0:
                        act.activation(PT[:, 4 * b:4 * b + 4:2, 0:r], ps[:, 0:4:2, 0:r], ACT.Copy).then_inc(S['pt_sb'], 1)
                    else:
                        act.activation(PT[:, 4 * b:4 * b + 4, :], ps, ACT.Copy).then_inc(S['pt_sb'], 1)

            def att_squares(i):
                r = ROWS[i]
                act.wait_ge(S['a_ready'], i + 1)
                act.activation(a_sq[0:r, :], atile[0:r, :], ACT.Square, accum_out=tiny[0:r, 64:65]).then_inc(S['ssa'], 1)

            act.wait_ge(S['ssm_made'], 1)
            att_exp(0)
            unit_evac(U, 'u_ps', 'u_sb')
            qkt_evac(5)
            unit_evac(Bst.rearrange("p a b c -> p (a b c)"), 'b_ps', 'b_sb')
            pt_evac(0)
            att_squares(0)
            att_exp(1)
            pt_evac(1)
            att_squares(1)
            att_exp(2)
            pt_evac(2)
            act.wait_ge(S['y_sb'], 6)
            act.activation(Y, Y, ACT.Gelu_apprx_tanh).then_inc(S['ssm_act'], 1)
            att_squares(2)
            att_exp(3)
            act.wait_ge(S['fin_ps'], 1)
            act.activation(finrow[0:16, :], bank[6][0:16, :], ACT.Copy).then_inc(S['fin_sb'], 1)
            act.wait_ge(S['z_sb'], 6)
            act.activation(Z, Z, ACT.Tanh, scale=0.5).then_inc(S['ssm_act'], 1)
            pt_evac(3)
            att_squares(3)
            att_exp(4)
            act.wait_ge(S['fin_out'], 64)
            for u in range(8):
                act.wait_ge(S['yt_ps'], u + 1)
                act.activation(yc[0:NCH, :, 64 * u:64 * u + 64].rearrange("p t (g q) -> p g t q", g=4),
                               bank[6 + u % 2][0:NCH, :].rearrange("p (g t q) -> p g t q", g=4, t=L), ACT.Copy
                               ).then_inc(S['yt_sb'], 1)
            pt_evac(4)
            att_squares(4)
            act.wait_ge(S['yt_sb'], 8)
            for s in range(L):
                if s:
                    act.wait_ge(S['ssy'], s)
                act.activation(Z[0:NCH, 0:512], yc[0:NCH, s, :], ACT.Square, accum_out=tiny[0:NCH, 16 + s:17 + s]
                               ).then_inc(S['ssy'], 1)
            act.wait_ge(S['ld_mem'], 64)
            for a in range(2):
                if a:
                    act.wait_ge(S['ssm_m'], a)
                act.activation(mem_sq, memx[:, a, :], ACT.Square, accum_out=tiny[:, 66 + a:67 + a]).then_inc(S['ssm_m'], 1)
            for u in range(8):
                k, th = divmod(u, 2)
                act.wait_ge(S['my_ps'], u + 1)
                dst = mixT[:, 4 + k, :].rearrange("p (c t) -> p c t", t=L)[:, :, 4 * th:4 * th + 4]
                act.activation(dst, bank[6 + u % 2][:, 0:4 * NCH].rearrange("p (t c) -> p c t", t=4), ACT.Identity,
                               scale=g_so[:, k:k + 1]).then_inc(S['my_sb'], 1)

            act.wait_ge(S['rms'], 2)
            for a in range(2):
                act.wait_ge(S['mk_ps'], a + 1)
                act.activation(mkt[a], bank[4 + a][:, :], ACT.Identity, scale=tiny[:, 68 + a:69 + a]).then_inc(S['mk_sb'], 1)

            def x1_squares(t):
                r = ROWS[t]
                act.wait_ge(S['x1'], T + t + 1)
                act.wait_ge(S['ssc'], t) if t else act.wait_ge(S['ssm_m'], 2)
                act.activation(mem_sq[0:r, :], x[0:r, t, :], ACT.Square, accum_out=tiny[0:r, 180 + t:181 + t]
                               ).then_inc(S['ssc'], 1)

            def mkT_evac(n):
                act.wait_ge(S['mkT_ps'], n + 1)
                if n == 0:
                    act.wait_ge(S['kout'], 64)
                act.activation(mkT[:, :, P * n:P * n + P], bank[4 + n % 2][:, :].rearrange("p (a b) -> p a b", a=4),
                               ACT.Copy).then_inc(S['mkT_sb'], 1)

            for t in range(3):
                x1_squares(t)
            mkT_evac(0)
            mkT_evac(1)
            x1_squares(3)
            x1_squares(4)
            for a in range(2):
                act.wait_ge(S['mv_ps'], a + 1)
                act.activation(mv[:, a, :], bank[6 + a][:, :], ACT.Identity, scale=tiny[:, 68 + a:69 + a]).then_inc(S['mv_sb'], 1)
            mkT_evac(2)
            mkT_evac(3)

            def cross_q(t):
                r = ROWS[t]
                act.wait_ge(S['cq_ps'], t + 1)
                if t == 0:
                    act.wait_ge(S['rms'], 3)
                rt_ = tiny[0:r, 185 + t:186 + t]
                if t < 4:
                    act.activation(qc[0:r, :], bank[2][0:r, :], ACT.Identity, scale=rt_).then_inc(S['cq_sb'], 1)
                else:
                    act.activation(qc[0:r, 0:256], bank[2][half_rows(t, 0), 0:256], ACT.Identity, scale=rt_)
                    act.activation(qc[0:r, 256:512], bank[2][half_rows(t, 1), 0:256], ACT.Identity, scale=rt_
                                   ).then_inc(S['cq_sb'], 1)

            def cross_qT(t):
                r = ROWS[t]
                act.wait_ge(S['cqT_ps'], t + 1)
                act.activation(qcT[:, :, 0:r], bank[3][:, :].rearrange("p (a b) -> p a b", a=4)[:, :, 0:r], ACT.Identity,
                               scale=gcol[:, 33:34]).then_inc(S['cqT_sb'], 1)

            def cross_exp(t):
                r = ROWS[t]
                act.wait_ge(S['cmax'], t + 1)
                for h in range(CAH):
                    act.activation(cP[0:r, h, :], bank[4 + h // 2][0:r, 256 * (h % 2):256 * (h % 2) + 256], ACT.Exp,
                                   bias=tiny[0:r, 72 + h:73 + h], accum_out=tiny[0:r, 76 + h:77 + h]).then_inc(S['cexp'], 1)

            def cross_out(t):
                r = ROWS[t]
                for b in range(2):
                    act.wait_ge(S['cp_ps'], 2 * t + b + 1)
                    act.activation(cPT[:, 4 * b:4 * b + 4, 0:r],
                                   bank[6 + b][:, :].rearrange("p (a b) -> p a b", a=4)[:, :, 0:r], ACT.Copy
                                   ).then_inc(S['cpt_sb'], 1)
                act.wait_ge(S['co_ps'], t + 1)
                act.activation(oT[:, :, 0:r], bank[3][:, :].rearrange("p (a b) -> p a b", a=4)[:, :, 0:r], ACT.Copy
                               ).then_inc(S['co_sb'], 1)

            cross_q(0)
            cross_qT(0)
            for t in range(T):
                cross_exp(t)
                if t < 4:
                    cross_q(t + 1)
                cross_out(t)
                if t < 4:
                    cross_qT(t + 1)

            act.wait_ge(S['cs_ps'], T)
            act.wait_ge(S['co_ps'], T)
            act.wait_ge(S['mem_out'], 64)
            act.dma_start(gffn, A['norm_ffn'][0].partition_broadcast(P)).then_inc(S['ld_wr'], 16)
            act.dma_start(crow, A['c_row']).then_inc(S['ld_wr'], 16)
            act.wait_ge(S['cw_ps'], T)
            for t in range(T):
                r = ROWS[t]
                act.wait_ge(S['x2'], t + 1)
                if t:
                    act.wait_ge(S['ssf'], t)
                act.activation(h3[0][0:r, :], x[0:r, t, :], ACT.Square, accum_out=tiny[0:r, 80 + t:81 + t]
                               ).then_inc(S['ssf'], 1)
            act.wait_ge(S['ssf'], T)
            act.wait_ge(S['rms'], 4)
            for t in range(4):
                act.activation(h3[t], x[:, t, :], ACT.Identity, scale=tiny[:, 85 + t:86 + t]).then_inc(S['h3a'], 1)
            act.wait_ge(S['lg_ps'], T)
            act.activation(h3[4][0:DEC, :], x[0:DEC, 4, :], ACT.Identity, scale=tiny[0:DEC, 89:90]).then_inc(S['h3a'], 1)
            act.wait_ge(S['asked'], 2)
            act.activation(rt[:, RT_EG:RT_EG + 20], rt[:, RT_EG:RT_EG + 20], ACT.Exp).then_inc(S['answered'], 1)
            act.wait_ge(S['asked'], 3)
            act.activation(rt[:, RT_D:RT_D + 5], rt[:, RT_D:RT_D + 5], ACT.Exp).then_inc(S['answered'], 1)

            def expert(jj, b):
                act.wait_ge(S['xgt_ps'], b + 1)
                act.activation(xgT[jj].rearrange("p a b -> p (a b)"), bank[jj][:, :], ACT.Copy).then_inc(S['xgt_sb'], 1)
                act.wait_ge(S['gu_used'], b + 1)
                if not isinstance(b, int) or b >= 1:
                    act.wait_ge(S['hact_ready'], b)
                act.activation(act1, bank[2 + jj][:, 0:256], ACT.Tanh, scale=0.5).then_inc(S['silu'], 1)
                act.wait_ge(S['ht_ps'], b + 1)
                if not isinstance(b, int) or b >= 1:
                    act.wait_ge(S['dn_used'], b)
                act.activation(hT.rearrange("p a b -> p (a b)"), bank[4][:, 0:256], ACT.Copy).then_inc(S['ht_sb'], 1)

            act.wait_ge(S['slots_ready'], 2)
            act.wait_ge(S['sc_done0'], 96)
            act.wait_ge(S['sc_done1'], 64)
            expert(0, 0)
            expert(1, 1)
            with act.Fori(1, 16) as it:
                for j in range(2):
                    expert(j, it * 2 + j)
            expert(0, 32)
            novf = act.value_load(ovf[0:1, N_OVF:N_OVF + 1], min_val=0, max_val=N_OVF)
            with act.If(novf > 1):
                with act.Fori(0, N_OVF - 1) as k:
                    with act.If(novf > k + 1):
                        act.wait_ge(S['xgt_ps'], k + 34)
                        act.activation(xgT[0].rearrange("p a b -> p (a b)"), bank[0][:, :], ACT.Copy).then_inc(S['xgt_sb'], 1)
                        act.wait_ge(S['gu_used'], k + 34)
                        act.wait_ge(S['hact_ready'], k + 33)
                        act.activation(act1, bank[2][:, 0:256], ACT.Tanh, scale=0.5).then_inc(S['silu'], 1)
                        act.wait_ge(S['ht_ps'], k + 34)
                        act.wait_ge(S['dn_used'], k + 33)
                        act.activation(hT.rearrange("p a b -> p (a b)"), bank[4][:, 0:256], ACT.Copy).then_inc(S['ht_sb'], 1)
                        act.wait_ge(S['y_ready'], k + 34)
                        for h in range(2):
                            act.dma_start(slots_out[bass.ds((k + 33) * CAP, CAP), h * 512:h * 512 + 512],
                                           yb[0][64 * h:64 * h + 64, :]).then_inc(S['y_more'], 16)
                        act.nop()
                    act.nop()
                act.nop()
            for t in range(T):
                r = ROWS[t]
                act.wait_ge(S['x3'], t + 1)
                dst = A['y_prompt'][0, TOK0[t]:TOK0[t] + r, :] if t < 4 else A['y_sample'][0]
                act.dma_start(dst, x[0:r, t, :]).then_inc(S['out_st'], 16)

        @block.vector
        def _(v):
            step = [0]

            def link(ins):
                step[0] += 1
                ins.then_inc(S['dve_step'], 1)
                v.wait_ge(S['dve_step'], step[0])

            def tt(o, a, b, op):
                link(v.tensor_tensor(o, a, b, op))

            def ts(o, a, s1, s2, o1, o2=ALU.bypass):
                link(v.tensor_scalar(o, a, s1, s2, o1, o2) if s2 is not None else v.tensor_scalar(o, a, s1, None, o1))

            def stt(o, a, s, b, o1, o2):
                link(v.scalar_tensor_tensor(o, a, s, b, o1, o2))

            def rsqrt(out, in_, scale, rows, n, s=None):
                a, y, t_ = rs_v[0:rows, 0:n], rs_y[0:rows, 0:n], rs_t[0:rows, 0:n]
                ts(a, in_, scale, EPS, ALU.mult, ALU.add)
                ts(y.bitcast(I32), a.bitcast(I32), -0.5, 1597463007.0, ALU.mult, ALU.add)
                for i in range(3):
                    stt(t_, y, -0.5, y, ALU.mult, ALU.mult)
                    tt(t_, t_, a, ALU.mult)
                    if i < 2 or s is None:
                        stt(out if i == 2 else y, t_, 1.5, y, ALU.add, ALU.mult)
                    else:
                        v.scalar_tensor_tensor(out, t_, 1.5, y, ALU.add, ALU.mult).then_inc(S[s], 1)

            def xt_evac(t):
                r = ROWS[t]
                for h in range(2):
                    v.wait_ge(S['xt_ps'], 2 * t + h + 1)
                    if t == 0 and h == 0:
                        v.wait_ge(S['ld_gain'], 16)
                    v.tensor_tensor(xT[:, 4 * h:4 * h + 4, TOK0[t]:TOK0[t] + r],
                                    bank[h][:, 0:4 * r].rearrange("p (a b) -> p a b", a=4),
                                    g_mix[:, 4 * h:4 * h + 4].unsqueeze(2).to_broadcast([P, 4, r]), ALU.mult
                                    ).then_inc(S['xt_sb'], 1)

            v.memset(tiny[:, :], 1.0).then_inc(S['dve_step'], 1)
            step[0] += 1
            v.wait_ge(S['dve_step'], step[0])
            v.memset(zero[:, :], 0.0).then_inc(S['cleared'], 1)
            xt_evac(0)
            v.wait_ge(S['ld_ssm'], 16 * 8)
            v.tensor_copy(smrow[0:16, 256:384].rearrange("p (a b) -> p a b", a=2),
                          smrow[0:16, 1024:1026].unsqueeze(2).to_broadcast([16, 2, 64]))
            link(v.tensor_copy(smrow[0:32, 768:896].rearrange("p (a b) -> p a b", a=8),
                               smrow[0:32, 1026:1042].unsqueeze(1).to_broadcast([32, 8, 16])))
            v.tensor_copy(smrow[0:32, 896:1024].rearrange("p (a b) -> p a b", a=8),
                          smrow[0:32, 1042:1058].unsqueeze(1).to_broadcast([32, 8, 16])).then_inc(S['sm'], 1)
            v.wait_ge(S['ssx'], T)
            rsqrt(tiny[:, 8:13], tiny[:, 0:5], 1.0 / DM, P, 5, 'rms')
            v.wait_ge(S['sm_ps'], 1)
            link(v.tensor_copy(ssm_s[:, 0:5, :].rearrange("p a b -> p (a b)"), bank[7][:, 0:80]))
            link(v.tensor_copy(Db[:, :, :].rearrange("p a b -> p (a b)"), bank[7][:, 128:192]))
            v.tensor_copy(g_so, bank[7][:, 192:196]).then_inc(S['sm'], 1)

            def constants():
                v.wait_ge(S['ld_const'], 16 * 12)
                link(v.tensor_copy(trib[:, 0:P], trif))
                v.memset(trib[:, P:2 * P], 1.0)
                link(v.tensor_copy(maskb[:, :], maskf[:, :]))
                ts(gqk[:, 0, :], gqk[:, 0, :], HD ** -0.5, None, ALU.mult)
                ts(gcol[:, 33:34], gcol[:, 32:33], CAD ** -0.5, None, ALU.mult)
                link(v.tensor_copy(sinkr[:, 1, :].rearrange("p (a b) -> p a b", a=2),
                                   sinkr[:, 0, :].rearrange("p (b a) -> p a b", a=2)))
                v.nop().then_inc(S['cst'], 1)

            q = lambda i: ssm_s[:, i, :]
            LR, LI, LDT, H0R, H0I = (q(i) for i in range(5))
            DT, SINA, COSA, SN_, CS_ = q(5), q(6), q(7), q(8), q(9)
            W1, W2, W3, EM1, RHO, RHO8, EC, ES, CR, CI, NR, NI = (q(i) for i in range(10, 22))

            def ssm_scalars():
                ts(W1, LDT, 1.0 / math.log(2.0), MAGIC, ALU.mult, ALU.add)
                ts(W1, W1, -MAGIC, None, ALU.add)
                stt(W2, W1, -0.693359375, LDT, ALU.mult, ALU.add)
                stt(W2, W2, 1.0, W2, ALU.mult, ALU.max)
                stt(W2, W1, 2.12194440054e-4, W2, ALU.mult, ALU.add)
                ts(W3, W2, 1.0 / 8, 1.0, ALU.mult, ALU.add)
                for k in range(7, 0, -1):
                    stt(W3, W3, 1.0 / k, W2, ALU.mult, ALU.mult)
                    ts(W3, W3, 1.0, None, ALU.add)
                ts(W1, W1, 127.0, 8388608.0, ALU.add, ALU.mult)
                link(v.tensor_copy(DT.bitcast(I32), W1))
                tt(DT, DT, W3, ALU.mult)
                tt(W1, LI, DT, ALU.mult)
                ts(W2, W1, 1.0 / (2 * math.pi), MAGIC, ALU.mult, ALU.add)
                ts(W2, W2, -MAGIC, None, ALU.add)
                stt(W1, W2, -6.28125, W1, ALU.mult, ALU.add)
                stt(W1, W2, -1.9353071795864769e-3, W1, ALU.mult, ALU.add)
                ts(SINA, W1, 3.1415925, -3.1415925, ALU.min, ALU.max)
                stt(W2, SINA, -1.0, SINA, ALU.mult, ALU.max)
                v.tensor_scalar(COSA, W2, -1.0, math.pi / 2, ALU.mult, ALU.add).then_inc(S['asked'], 1)
                tt(W1, LR, DT, ALU.mult)
                ts(W1, W1, 1.0 / 16, -1.0, ALU.mult, ALU.max)
                ts(W2, W1, 1.0 / 9, 1.0, ALU.mult, ALU.add)
                for k in range(8, 1, -1):
                    stt(W2, W2, 1.0 / k, W1, ALU.mult, ALU.mult)
                    ts(W2, W2, 1.0, None, ALU.add)
                tt(EM1, W2, W1, ALU.mult)
                for _ in range(4):
                    stt(EM1, EM1, 2.0, EM1, ALU.add, ALU.mult)
                ts(RHO, EM1, 1.0, None, ALU.add)
                stt(W1, EM1, 2.0, EM1, ALU.add, ALU.mult)
                stt(W2, W1, 2.0, W1, ALU.add, ALU.mult)
                stt(W1, W2, 2.0, W2, ALU.add, ALU.mult)
                ts(RHO8, W1, 1.0, None, ALU.add)
                v.wait_ge(S['answered'], 1)
                tt(powj[:, 0, :, 1], RHO, CS_, ALU.mult)
                tt(powj[:, 1, :, 1], RHO, SN_, ALU.mult)
                tt(NR, EM1, CS_, ALU.mult)
                stt(NR, CS_, -1.0, NR, ALU.add, ALU.add)
                link(v.tensor_copy(NI, powj[:, 1, :, 1]))
                tt(W1, LR, LR, ALU.mult)
                tt(W2, LI, LI, ALU.mult)
                tt(W1, W1, W2, ALU.add)
                link(v.reciprocal(W3, W1))
                tt(W1, NR, LR, ALU.mult)
                tt(W2, NI, LI, ALU.mult)
                tt(W1, W1, W2, ALU.add)
                tt(CR, W1, W3, ALU.mult)
                tt(W1, NI, LR, ALU.mult)
                tt(W2, NR, LI, ALU.mult)
                tt(W1, W1, W2, ALU.subtract)
                tt(CI, W1, W3, ALU.mult)
                v.memset(powj[:, 0, :, 0], 1.0)
                link(v.memset(powj[:, 1, :, 0], 0.0))
                def cmul(o, lo, n, src, m):
                    a_, b_ = powj[:, 0, :, src:src + n], powj[:, 1, :, src:src + n]
                    c_ = powj[:, 0, :, m:m + 1].to_broadcast([P, NPAIR, n])
                    d_ = powj[:, 1, :, m:m + 1].to_broadcast([P, NPAIR, n])
                    t1, t2 = (vtmp[:, 64 * i:64 * i + NPAIR * n].rearrange("p (a b) -> p a b", b=n) for i in range(2))
                    tt(t1, a_, c_, ALU.mult)
                    tt(t2, b_, d_, ALU.mult)
                    tt(powj[:, 0, :, o:o + n], t1, t2, ALU.subtract)
                    tt(t1, a_, d_, ALU.mult)
                    tt(t2, b_, c_, ALU.mult)
                    tt(powj[:, 1, :, o:o + n], t1, t2, ALU.add)
                cmul(2, 0, 1, 1, 1)
                cmul(3, 0, 2, 1, 2)
                cmul(5, 0, 4, 1, 4)
                for g2 in range(2):
                    rows = slice(64 * g2, 64 * g2 + 64)
                    for c in range(2):
                        top = slice(64 * c, 64 * c + 64)
                        ps = powS.rearrange("p i (a g) j -> p i g a j", g=2)
                        v.tensor_copy(ps[top, 0, g2], powj[rows, 0])
                        m = v.tensor_scalar(ps[top, 1, g2], powj[rows, 1], 1.0 - 2.0 * c, None, ALU.mult)
                v.wait_ge(S['c_sb'], 2)
                link(m)
                v.nop().then_inc(S['pow_ready'], 1)

            def ssm_b():
                v.wait_ge(S['ld_b'], 32)
                cr = CR.unsqueeze(2).to_broadcast([P, NPAIR, SG])
                ci = CI.unsqueeze(2).to_broadcast([P, NPAIR, SG])
                t1 = vtmp[:, 0:256].rearrange("p (a b) -> p a b", a=NPAIR)
                tt(t1, Braw[:, 1], ci, ALU.mult)
                tt(Bb[:, 0], Braw[:, 0], cr, ALU.mult)
                tt(Bb[:, 0], Bb[:, 0], t1, ALU.subtract)
                tt(t1, Braw[:, 0], ci, ALU.mult)
                tt(Bb[:, 1], Braw[:, 1], cr, ALU.mult)
                tt(Bb[:, 1], Bb[:, 1], t1, ALU.add)
                for s in range(L):
                    m = v.tensor_copy(powr[:, :, :, s], powj[:, :, :, L - 1 - s])
                link(m)
                bs = BbS.rearrange("p (a g) q -> p g a q", g=2)
                for g2 in range(2):
                    for c in range(2):
                        m = v.tensor_copy(bs[64 * c:64 * c + 64, g2], Bb[64 * g2:64 * g2 + 64, c])
                link(m)
                v.nop().then_inc(S['bb_ready'], 1)

            def c_evac(a):
                v.wait_ge(S['c_ps'], a + 1)
                ps = bank[7][:, :].rearrange("p (g q) -> p g q", q=SG)
                f_ = 1.0 if a == 0 else -1.0
                v.tensor_scalar(CS[0:64, a], ps[0:64], f_, None, ALU.mult)
                v.tensor_scalar(CS[64:128, 1 - a], ps[64:128], f_, None, ALU.mult).then_inc(S['c_sb'], 1)

            def ssm_wb():
                shp = [P, NPAIR, L, SG]
                e = lambda z: z.unsqueeze(3).to_broadcast(shp)
                f = lambda z: z.unsqueeze(2).to_broadcast(shp)
                o4 = [WB[:, i].rearrange("p a (n m) -> p a n m", m=SG) for i in range(2)]
                t4 = wbtmp.rearrange("p (a n m) -> p a n m", a=NPAIR, n=L)
                tt(t4, e(powr[:, 1]), f(Bb[:, 1]), ALU.mult)
                tt(o4[0], e(powr[:, 0]), f(Bb[:, 0]), ALU.mult)
                tt(o4[0], o4[0], t4, ALU.subtract)
                tt(t4, e(powr[:, 1]), f(Bb[:, 0]), ALU.mult)
                tt(o4[1], e(powr[:, 0]), f(Bb[:, 1]), ALU.mult)
                v.tensor_tensor(o4[1], o4[1], t4, ALU.add).then_inc(S['wb_ready'], 1)

            def qk_norm(t):
                r = ROWS[t]
                v.wait_ge(S['proj_sb'], t + 1)
                tt(sq[0:r, :], qk[0:r, :], qk[0:r, :], ALU.mult)
                link(v.tensor_reduce(tiny[0:r, 90:100], sq[0:r, :].rearrange("p (a b) -> p a b", a=10), AX.X, ALU.add))
                rsqrt(tiny[0:r, 100:110], tiny[0:r, 90:100], 1.0 / HD, r, 10)
                q3 = qk[0:r, :].rearrange("p (a b) -> p a b", a=10)
                s3 = sq[0:r, :].rearrange("p (a b) -> p a b", a=10)
                tt(s3, q3, tiny[0:r, 100:110].unsqueeze(2).to_broadcast([r, 10, HD]), ALU.mult)
                v.tensor_tensor(q3[:, 0:8], s3[:, 0:8], gqk[0:r, 0:1, :].to_broadcast([r, 8, HD]), ALU.mult)
                tt(q3[:, 8:10], s3[:, 8:10], gqk[0:r, 1:2, :].to_broadcast([r, 2, HD]), ALU.mult)
                cc = rope[0:r, t, 0:1, :].to_broadcast([r, 10, 16])
                s_lo = rope[0:r, t, 1:2, 0:8].to_broadcast([r, 10, 8])
                s_hi = rope[0:r, t, 1:2, 8:16].to_broadcast([r, 10, 8])
                tb = s3[:, :, 16:32]
                v.tensor_tensor(tb[:, :, 0:8], q3[:, :, 8:16], s_lo, ALU.mult)
                v.tensor_tensor(tb[:, :, 8:16], q3[:, :, 0:8], s_hi, ALU.mult)
                tt(s3[:, :, 0:16], q3[:, :, 0:16], cc, ALU.mult)
                tt(q3[:, :, 0:16], s3[:, :, 0:16], tb, ALU.add)
                v.tensor_copy(kdup[0:r, :, :].rearrange("p (a d) n -> p a d n", d=2),
                              q3[:, 8:10, :].unsqueeze(2).to_broadcast([r, 2, 2, HD])).then_inc(S['qk_ready'], 1)

            xt_evac(1)
            c_evac(0)
            c_evac(1)
            xt_evac(2)
            constants()
            qk_norm(0)
            ssm_scalars()
            xt_evac(3)
            qk_norm(1)
            ssm_b()
            xt_evac(4)
            qk_norm(2)
            ssm_wb()
            qk_norm(3)
            qk_norm(4)
            v.wait_ge(S['uc_ld'], 16)
            v.tensor_copy(ucg[0:NCH].rearrange("p (g b) (s q) -> p b g s q", b=2, q=SG)[:, 0],
                          uc[0:NCH].rearrange("p s (g b q) -> p b g s q", b=2, q=SG)[:, 0]).then_inc(S['ucg'], 1)

            Br, Bi = Bst[:, 0], Bst[:, 1]
            fl = lambda z: z.rearrange("p a b -> p (a b)")
            Tc, Ts, Brf, Bif = fl(Trot[:, 0]), fl(Trot[:, 1]), fl(Br), fl(Bi)
            X1, X2 = rot[:, 0].rearrange("p (a b) -> p a b", a=NPAIR), rot[:, 1].rearrange("p (a b) -> p a b", a=NPAIR)

            def scan_tables():
                v.wait_ge(S['ssm_made'], 1)
                link(v.tensor_copy(EC, CS_))
                link(v.tensor_copy(ES, SN_))

                def square():
                    v.tensor_tensor(W1, EC, EC, ALU.mult)
                    tt(W2, ES, ES, ALU.mult)
                    stt(ES, EC, 2.0, ES, ALU.mult, ALU.mult)
                    tt(EC, W1, W2, ALU.subtract)

                for _ in range(3):
                    square()
                v.memset(Trot[:, 0, :, 0], 1.0)
                link(v.memset(Trot[:, 1, :, 0], 0.0))
                n = 1
                while n < NCH_P:
                    c_, s_ = Trot[:, 0, :, 0:n], Trot[:, 1, :, 0:n]
                    e_c = EC.unsqueeze(2).to_broadcast([P, NPAIR, n])
                    e_s = ES.unsqueeze(2).to_broadcast([P, NPAIR, n])
                    t1, t2 = (R8.rearrange("p a b -> p (a b)")[:, 512 * i:512 * i + NPAIR * n].rearrange(
                        "p (a b) -> p a b", b=n) for i in range(2))
                    v.tensor_tensor(t1, s_, e_s, ALU.mult)
                    v.tensor_tensor(t2, s_, e_c, ALU.mult)
                    v.tensor_tensor(Trot[:, 0, :, n:2 * n], c_, e_c, ALU.mult)
                    tt(Trot[:, 1, :, n:2 * n], c_, e_s, ALU.mult)
                    v.tensor_tensor(Trot[:, 0, :, n:2 * n], Trot[:, 0, :, n:2 * n], t1, ALU.subtract)
                    tt(Trot[:, 1, :, n:2 * n], Trot[:, 1, :, n:2 * n], t2, ALU.add)
                    square()
                    n *= 2
                v.tensor_copy(Trot[:, :, :, NCH_P:NCH], Trot[:, :, :, 0:NCH_S])
                link(v.tensor_copy(R8[:, :, :], RHO8.unsqueeze(2).to_broadcast([P, NPAIR, NCH])))
                link(v.memset(R8[:, :, 0:NCH:NCH_P], 0.0))

            def scan_in():
                v.wait_ge(S['b_sb'], 6)
                mr, mi = powj[:, 0, :, 8], powj[:, 1, :, 8]
                for dst, a_, b_, op in ((Br, H0R, H0I, ALU.subtract), (Bi, H0I, H0R, ALU.add)):
                    tt(W1, mr, a_, ALU.mult)
                    tt(W2, mi, b_, ALU.mult)
                    tt(W1, W1, W2, op)
                    tt(dst[:, :, NCH_P], dst[:, :, NCH_P], W1, ALU.add)
                v.tensor_tensor(Htmp[:, 0], Bif, Ts, ALU.mult)
                tt(Htmp[:, 1], Brf, Ts, ALU.mult)
                v.tensor_tensor(Brf, Brf, Tc, ALU.mult)
                tt(Bif, Bif, Tc, ALU.mult)
                v.tensor_tensor(Brf, Brf, Htmp[:, 0], ALU.add)
                tt(Bif, Bif, Htmp[:, 1], ALU.subtract)

            def states(c, op):
                for g2 in range(2):
                    rows = slice(64 * g2, 64 * g2 + 64)
                    m = v.tensor_tensor(H[64 * c:64 * c + 64, 16 * g2:16 * g2 + 16, 1:NCH + 1], X1[rows], X2[rows], op)
                link(m)

            def scan():
                v.tensor_tensor_scan(Brf, fl(R8), Brf, 0.0, ALU.mult, ALU.add)
                link(v.tensor_tensor_scan(Bif, fl(R8), Bif, 0.0, ALU.mult, ALU.add))
                v.tensor_tensor(X1, Br, Trot[:, 0], ALU.mult)
                tt(X2, Bi, Trot[:, 1], ALU.mult)
                states(0, ALU.subtract)

            def scan_out():
                v.tensor_tensor(X1, Bi, Trot[:, 0], ALU.mult)
                tt(X2, Br, Trot[:, 1], ALU.mult)
                states(1, ALU.add)
                for c, h0 in enumerate((H0R, H0I)):
                    for g2 in range(2):
                        h_ = H[64 * c:64 * c + 64, 16 * g2:16 * g2 + 16]
                        rows = slice(64 * g2, 64 * g2 + 64)
                        link(v.tensor_copy(fin[rows, c:4:2, :], h_[:, :, NCH_P:NCH + 1:NCH_S].rearrange("p a s -> p s a")))
                        link(v.tensor_copy(h_[:, :, NCH_P], h0[rows]))
                link(v.memset(H[:, :, 0], 0.0))
                Yv = Y.rearrange("p (g a c) -> p g a c", g=2, a=NPAIR)
                Uv = U.rearrange("p (g a c) -> p g a c", g=2, a=NPAIR)
                Dv = Db[:, 0, :].rearrange("p (a g) -> p g a", g=2).unsqueeze(3).to_broadcast([P, 2, NPAIR, NCH])
                v.tensor_tensor(Yv, Uv, Dv, ALU.mult).then_inc(S['h_ready'], 1)
                v.wait_ge(S['h_ready'], 1)

            def y_add():
                for u, (lo, hi) in enumerate(UNITS):
                    v.wait_ge(S['y_ps'], u + 1)
                    v.tensor_tensor(Y[:, lo * NCH:hi * NCH], Y[:, lo * NCH:hi * NCH], bank[6 + u % 2][:, 0:(hi - lo) * NCH],
                                    ALU.add).then_inc(S['y_sb'], 1)

            def z_add():
                bv = Db[:, 1, :].rearrange("p (a g) -> p g a", g=2)
                for u, (lo, hi) in enumerate(UNITS):
                    g2, a0 = divmod(lo, 16)
                    n = hi - lo
                    v.wait_ge(S['z_ps'], u + 1)
                    v.tensor_tensor(Z[:, lo * NCH:hi * NCH].rearrange("p (a c) -> p a c", a=n),
                                    bank[6 + u % 2][:, 0:n * NCH].rearrange("p (a c) -> p a c", a=n),
                                    bv[:, g2, a0:a0 + n].unsqueeze(2).to_broadcast([P, n, NCH]), ALU.add).then_inc(S['z_sb'], 1)

            def glu():
                v.wait_ge(S['ssm_act'], 2)
                v.scalar_tensor_tensor(Y, Z, 1.0, Y, ALU.add, ALU.mult).then_inc(S['glu_done'], 1)

            def y_norm():
                v.wait_ge(S['ssy'], 8)
                rsqrt(tiny[0:NCH, 24:32], tiny[0:NCH, 16:24], 0.25 / 512, NCH, 8)
                ts(tiny[0:NCH, 24:32], tiny[0:NCH, 24:32], 0.5, None, ALU.mult)
                for s in range(L):
                    v.tensor_scalar(yc[0:NCH, s, :], yc[0:NCH, s, :], tiny[0:NCH, 24 + s:25 + s], None, ALU.mult
                                    ).then_inc(S['yn'], 1)

            def att_max(i):
                r = ROWS[i]
                w = P if i == 0 else 192 if i == 4 else 256
                v.wait_ge(S['s_ps'], i + 1)
                if i:
                    v.wait_ge(S['expd'], 9 * i)
                for b in range(4):
                    m = v.tensor_reduce(tiny[0:r, 110 + 2 * b:112 + 2 * b],
                                        bank[b][0:r, :].rearrange("p (a b) -> p a b", a=2)[:, :, 0:w], AX.X, ALU.max)
                link(m)
                tt(tiny[0:r, 120:128], tiny[0:r, 110:118], sinkr[0:r, 1, :], ALU.max)
                ts(tiny[0:r, 32:40], tiny[0:r, 120:128], -1.0, None, ALU.mult)
                v.tensor_tensor(tiny[0:r, 40:48], tiny[0:r, 32:40], sinkr[0:r, 1, :], ALU.add).then_inc(S['nmax'], 1)

            def att_denominator(i):
                r = ROWS[i]
                v.wait_ge(S['expd'], 9 * i + 9)
                tt(tiny[0:r, 130:138], tiny[0:r, 56:64], tiny[0:r, 48:56], ALU.add)
                link(v.reciprocal(tiny[0:r, 140:148], tiny[0:r, 130:138]))

            def att_rows(i):
                r = ROWS[i]
                v.wait_ge(S['o_ps'], i + 1)
                if i:
                    v.wait_ge(S['at_ps'], i)
                av = atile[0:r, :].rearrange("p (b a d) -> p a b d", a=2, d=HD)
                for a in range(2):
                    m = v.tensor_tensor(av[:, a], bank[4][0:r, 256 * a:256 * a + 256].rearrange("p (b d) -> p b d", b=4),
                                        tiny[0:r, 140 + 4 * a:144 + 4 * a].unsqueeze(2).to_broadcast([r, 4, HD]), ALU.mult)
                m.then_inc(S['a_ready'], 1)

            def att_norm(i):
                r = ROWS[i]
                v.wait_ge(S['ssa'], i + 1)
                rsqrt(tiny[0:r, 65:66], tiny[0:r, 64:65], 1.0 / 512, r, 1)
                v.tensor_scalar(atile[0:r, :], atile[0:r, :], tiny[0:r, 65:66], None, ALU.mult).then_inc(S['a_norm'], 1)

            def att_T(i):
                r = ROWS[i]
                v.wait_ge(S['at_ps'], i + 1)
                v.tensor_tensor(mixT[:, 0:4, TOK0[i]:TOK0[i] + r],
                                bank[5][:, 0:4 * r].rearrange("p (a b) -> p a b", a=4),
                                g_ao.unsqueeze(2).to_broadcast([P, 4, r]), ALU.mult).then_inc(S['at_sb'], 1)

            def x1_add(n):
                half, t = divmod(n, T)
                b = 4 if half == 0 else 2 * (t % 2)
                r = ROWS[t]
                v.wait_ge(S['wo_ps'], n + 1)
                for h in range(2):
                    m = v.tensor_tensor(x[0:r, t, 512 * h:512 * h + 512], x[0:r, t, 512 * h:512 * h + 512],
                                        bank[b + h][half_rows(t, h), :], ALU.add)
                m.then_inc(S['x1'], 1)

            att_max(0)
            scan_tables()
            scan_in()
            att_denominator(0)
            v.wait_ge(S['kout'], 64)
            att_rows(0)
            att_norm(0)
            att_max(1)
            att_T(0)
            scan()
            x1_add(0)
            att_denominator(1)
            att_rows(1)
            att_norm(1)
            att_max(2)
            att_T(1)
            scan_out()
            x1_add(1)
            y_add()
            att_denominator(2)
            att_rows(2)
            att_norm(2)
            att_max(3)
            att_T(2)
            x1_add(2)
            z_add()
            glu()
            att_denominator(3)
            att_rows(3)
            att_norm(3)
            att_max(4)
            att_T(3)
            x1_add(3)
            att_denominator(4)
            att_rows(4)
            att_norm(4)
            att_T(4)
            y_norm()
            x1_add(4)

            v.wait_ge(S['ssm_m'], 2)
            rsqrt(tiny[:, 68:70], tiny[:, 66:68], 1.0 / DM, P, 2, 'rms')
            for a in range(2):
                for h in range(2):
                    n = 2 * a + h
                    v.wait_ge(S['mt_ps'], n + 1)
                    v.tensor_tensor(memT[:, 4 * h:4 * h + 4, P * a:P * a + P],
                                    bank[n][:, :].rearrange("p (a b) -> p a b", a=4),
                                    g_mem[:, 4 * h:4 * h + 4].unsqueeze(2).to_broadcast([P, 4, P]), ALU.mult
                                    ).then_inc(S['mt_sb'], 1)

            def mk_norm(a):
                v.wait_ge(S['mk_sb'], a + 1)
                if a:
                    v.wait_ge(S['mkn'], a)
                mk3 = mkt[a].rearrange("p (a b) -> p a b", a=CAH)
                ms3 = mksq.rearrange("p (a b) -> p a b", a=CAH)
                tt(mksq, mkt[a], mkt[a], ALU.mult)
                link(v.tensor_reduce(tiny[:, 150:154], ms3, AX.X, ALU.add))
                rsqrt(tiny[:, 154:158], tiny[:, 150:154], 1.0 / CAD, P, 4)
                tt(ms3, mk3, tiny[:, 154:158].unsqueeze(2).to_broadcast([P, CAH, CAD]), ALU.mult)
                v.tensor_tensor(mk3, ms3, gck[:, :].unsqueeze(1).to_broadcast([P, CAH, CAD]), ALU.mult).then_inc(S['mkn'], 1)

            mk_norm(0)
            x1_add(5)
            mk_norm(1)
            for n in range(6, 10):
                x1_add(n)
            v.wait_ge(S['ssc'], T)
            rsqrt(tiny[:, 185:190], tiny[:, 180:185], 1.0 / DM, P, 5, 'rms')

            def cross_x(t):
                r = ROWS[t]
                for h in range(2):
                    v.wait_ge(S['xt_ps'], 2 * (T + t) + h + 1)
                    v.tensor_tensor(x1T[:, 4 * h:4 * h + 4, 0:r], bank[h][:, 0:4 * r].rearrange("p (a b) -> p a b", a=4),
                                    g_cross[:, 4 * h:4 * h + 4].unsqueeze(2).to_broadcast([P, 4, r]), ALU.mult
                                    ).then_inc(S['xt_sb'], 1)

            def cross_q(t):
                r = ROWS[t]
                v.wait_ge(S['cq_sb'], t + 1)
                q3 = qc[0:r, :].rearrange("p (a b) -> p a b", a=CAH)
                s3 = x1T.rearrange("p a b -> p (a b)")[0:r, 0:512].rearrange("p (a b) -> p a b", a=CAH)
                tt(s3, q3, q3, ALU.mult)
                link(v.tensor_reduce(tiny[0:r, 160:164], s3, AX.X, ALU.add))
                rsqrt(tiny[0:r, 164:168], tiny[0:r, 160:164], 1.0 / CAD, r, 4)
                v.tensor_tensor(q3, q3, tiny[0:r, 164:168].unsqueeze(2).to_broadcast([r, CAH, CAD]), ALU.mult
                                ).then_inc(S['cqn'], 1)

            def cross_max(t):
                r = ROWS[t]
                v.wait_ge(S['cs_ps'], t + 1)
                for b in range(2):
                    m = v.tensor_reduce(tiny[0:r, 170 + 2 * b:172 + 2 * b],
                                        bank[4 + b][0:r, :].rearrange("p (a b) -> p a b", a=2), AX.X, ALU.max)
                link(m)
                v.tensor_scalar(tiny[0:r, 72:76], tiny[0:r, 170:174], -1.0, None, ALU.mult).then_inc(S['cmax'], 1)

            def cross_p(t):
                r = ROWS[t]
                v.wait_ge(S['cexp'], 4 * t + 4)
                link(v.reciprocal(tiny[0:r, 176:180], tiny[0:r, 76:80]))
                v.tensor_tensor(cP[0:r], cP[0:r], tiny[0:r, 176:180].unsqueeze(2).to_broadcast([r, CAH, 256]), ALU.mult
                                ).then_inc(S['cpn'], 1)

            def x2_add(t):
                r = ROWS[t]
                v.wait_ge(S['cw_ps'], t + 1)
                for h in range(2):
                    m = v.tensor_tensor(x[0:r, t, 512 * h:512 * h + 512], x[0:r, t, 512 * h:512 * h + 512],
                                        bank[h][half_rows(t, h), :], ALU.add)
                m.then_inc(S['x2'], 1)

            cross_x(0)
            cross_q(0)
            for t in range(T):
                cross_max(t)
                if t < 4:
                    cross_x(t + 1)
                cross_p(t)
                if t < 4:
                    cross_q(t + 1)
                x2_add(t)

            def route():
                def f(lo, *dims):
                    n = int(np.prod(dims))
                    w_ = rt[:, lo:lo + n]
                    if len(dims) == 1:
                        return w_
                    nm = "abc"[:len(dims)]
                    return w_.rearrange(f"p ({' '.join(nm)}) -> p {' '.join(nm)}", **dict(zip(nm, dims)))

                def bc(a, *shape):
                    return a.to_broadcast([P, *shape])

                Lg = f(0, T, 36)
                v.wait_ge(S['mem_out'], 64)
                link(v.memset(rt[:, 0:180], 0.0))
                v.wait_ge(S['lg_ps'], T)
                v.tensor_tensor(Lg[:, 0:4, :], bank[4][:, 0:144].rearrange("p (a b) -> p a b", a=4),
                                tiny[:, 85:89].unsqueeze(2).to_broadcast([P, 4, 36]), ALU.mult)
                tt(Lg[0:DEC, 4, :], bank[4][0:DEC, 144:180], tiny[0:DEC, 89:90].to_broadcast([DEC, 36]), ALU.mult)
                v.tensor_tensor(Lg[:, 0:4, :], Lg[:, 0:4, :], bc(brt.unsqueeze(1), 4, 36), ALU.add)
                tt(Lg[0:DEC, 4, :], Lg[0:DEC, 4, :], brt[0:DEC, :], ALU.add)
                lg, le = Lg[:, :, 0:4], Lg[:, :, 4:36]
                gm, eg, sg, pg = f(180, T), f(RT_EG, T, 4), f(205, T), f(210, T)

                def top(src, n, m, score, c, hot):
                    link(v.tensor_reduce(m, src, AX.X, ALU.max))
                    tt(score, src, bc(m.unsqueeze(2), T, n), ALU.is_ge)
                    tt(score, score, bc(c.unsqueeze(1), T, n), ALU.mult)
                    link(v.tensor_reduce(f(255, T), score, AX.X, ALU.max))
                    tt(hot, score, bc(f(255, T).unsqueeze(2), T, n), ALU.is_equal)

                ghot = f(215, T, 4)
                top(lg, 4, gm, f(235, T, 4), crow[:, 0:4], ghot)
                v.tensor_tensor(eg, lg, bc(gm.unsqueeze(2), T, 4), ALU.subtract).then_inc(S['asked'], 1)
                prod = f(810, T, 4, 8)
                le4 = le.rearrange("p t (g e) -> p t g e", g=4)
                tt(prod, le4, bc(ghot.unsqueeze(3), T, 4, 8), ALU.mult)
                lesel, m1, hot1, le2, m2, hot2 = f(260, T, 8), f(300, T), f(305, T, 8), f(385, T, 8), f(425, T), f(430, T, 8)
                link(v.tensor_reduce(lesel, prod.rearrange("p t g e -> p t e g"), AX.X, ALU.add))
                top(lesel, 8, m1, f(345, T, 8), crow[:, 4:12], hot1)
                stt(le2, hot1, -1e30, lesel, ALU.mult, ALU.add)
                top(le2, 8, m2, f(345, T, 8), crow[:, 4:12], hot2)
                d, rd, g1, g2 = f(RT_D, T), f(475, T), f(RT_G1, T), f(RT_G2, T)
                v.tensor_tensor(d, m2, m1, ALU.subtract).then_inc(S['asked'], 1)
                ho = [f(490, T, 4, 8), f(650, T, 4, 8)]
                v.tensor_tensor(ho[0], bc(ghot.unsqueeze(3), T, 4, 8), bc(hot1.unsqueeze(2), T, 4, 8), ALU.mult)
                tt(ho[1], bc(ghot.unsqueeze(3), T, 4, 8), bc(hot2.unsqueeze(2), T, 4, 8), ALU.mult)
                v.memset(rt[DEC:P, 490 + 128:490 + 160], 0.0)
                link(v.memset(rt[DEC:P, 650 + 128:650 + 160], 0.0))
                v.tensor_tensor(hotb, rt[:, 490:650], rt[:, 650:810], ALU.add).then_inc(S['oh_ready'], 1)
                v.wait_ge(S['cnt_ps'], 1)
                rank, base, ne, ov, inc = f(970, T, NEXP), f(1130, NEXP), f(1162, NEXP), f(1194, NEXP), f(1226, NEXP)
                before = bank[5][:, 0:160].rearrange("p (a b) -> p a b", a=T)
                total = bank[6][:, 0:160].rearrange("p (a b) -> p a b", a=T)
                v.tensor_copy(rank[:, 0, :], before[:, 0, :])
                so_far = [ne, ov]
                link(v.tensor_copy(ne, total[:, 0, :]))
                for t in range(1, T):
                    v.tensor_tensor(rank[:, t, :], before[:, t, :], so_far[(t - 1) % 2], ALU.add)
                    tt(so_far[t % 2], so_far[(t - 1) % 2], total[:, t, :], ALU.add)
                c8 = rtmp[:, 0:256].rearrange("p (a b) -> p a b", a=NEXP)
                tt(c8, bc(ne.unsqueeze(2), NEXP, 8), bc(crow[:, 12:20].unsqueeze(1), NEXP, 8), ALU.is_gt)
                link(v.tensor_reduce(ov, c8, AX.X, ALU.add))
                link(v.tensor_tensor_scan(inc, zero[:, 0:NEXP], ov, 0.0, ALU.add, ALU.add))
                tt(base, inc, ov, ALU.subtract)
                stt(base, base, 64.0, crow[:, 52:84], ALU.mult, ALU.add)
                over = f(810, T, NEXP)
                ts(over, rank, float(CAP), None, ALU.is_ge)
                tt(over, over, bc(base.unsqueeze(1), T, NEXP), ALU.mult)
                tt(over, over, rank, ALU.add)
                tt(over, over, bc(crow[:, 20:52].unsqueeze(1), T, NEXP), ALU.add)
                for c, lo in ((0, 490), (1, 650)):
                    m = v.tensor_tensor(f(lo, T, NEXP), f(lo, T, NEXP), over, ALU.mult)
                link(m)
                for c, lo in ((0, 490), (1, 650)):
                    m = v.tensor_reduce(f(260 + T * c, T), f(lo, T, NEXP), AX.X, ALU.add)
                link(m)
                v.tensor_copy(idx[:, :], f(260, 2 * T)).then_inc(S['slots_ready'], 1)
                v.wait_ge(S['slots_ready'], 1)
                c17 = rtmp.rearrange("p (a b) -> p a b", a=N_OVF)
                tt(c17, bc(inc.unsqueeze(1), N_OVF, NEXP), bc(crow[:, 84:101].unsqueeze(2), N_OVF, NEXP), ALU.is_le)
                link(v.tensor_reduce(f(0, N_OVF), c17, AX.X, ALU.add))
                ts(f(0, N_OVF), f(0, N_OVF), float(NEXP - 1), None, ALU.min)
                link(v.tensor_copy(ovf[:, 0:N_OVF], f(0, N_OVF)))
                v.tensor_copy(ovf[:, N_OVF:N_OVF + 1], inc[:, NEXP - 1:NEXP]).then_inc(S['slots_ready'], 1)
                v.wait_ge(S['answered'], 3)
                link(v.tensor_reduce(sg, eg, AX.X, ALU.add))
                v.reciprocal(pg, sg)
                ts(rd, d, 1.0, None, ALU.add)
                link(v.reciprocal(rd, rd))
                tt(g1, pg, rd, ALU.mult)
                tt(g2, g1, d, ALU.mult)

            for t in range(T):
                r = ROWS[t]
                for h in range(2):
                    v.wait_ge(S['h3T_ps'], 2 * t + h + 1)
                    if t == 0 and h == 0:
                        v.wait_ge(S['cw_ps'], T)
                    if t and h == 0:
                        v.wait_ge(S['lg_ps'], t)
                    v.tensor_tensor(x2T[:, 4 * h:4 * h + 4, 0:r], bank[2 * (t % 2) + h][:, 0:4 * r].rearrange("p (a b) -> p a b", a=4),
                                    g_ffn[:, 4 * h:4 * h + 4].unsqueeze(2).to_broadcast([P, 4, r]), ALU.mult
                                    ).then_inc(S['h3T_sb'], 1)
                if t == 1:
                    v.wait_ge(S['ssf'], T)
                    rsqrt(tiny[:, 85:90], tiny[:, 80:85], 1.0 / DM, P, 5, 'rms')
            v.wait_ge(S['rms'], 4)
            route()
            v.wait_ge(S['sc_done0'], 96)
            v.wait_ge(S['sc_done1'], 64)

            def expert(jj, b, n_out):
                v.wait_ge(S['silu'], b + 1)
                v.scalar_tensor_tensor(act1, act1, 1.0, bank[2 + jj][:, 0:256], ALU.add, ALU.mult).then_inc(S['gated'], 1)
                v.wait_ge(S['gated'], b + 1)
                if not isinstance(b, int) or b >= 1:
                    v.wait_ge(S['ht_ps'], b)
                v.scalar_tensor_tensor(hact, act1, 0.5, bank[2 + jj][:, 256:512], ALU.mult, ALU.mult
                                       ).then_inc(S['hact_ready'], 1)
                v.wait_ge(S['dn_used'], b + 1)
                if n_out is not None:
                    v.wait_ge(S[f'y_out{jj}'], n_out)
                v.tensor_copy(yb[jj], bank[6 + jj][:, :]).then_inc(S['y_ready'], 1)

            expert(0, 0, None)
            expert(1, 1, None)
            with v.Fori(1, 16) as it:
                for j in range(2):
                    expert(j, it * 2 + j, it * 32)
            expert(0, 32, 32 * 16)
            novf = v.value_load(ovf[0:1, N_OVF:N_OVF + 1], min_val=0, max_val=N_OVF)
            v.wait_ge(S['y_out0'], 32 * 17)
            v.nop().then_inc(S['v_go'], 1)
            with v.If(novf > 1):
                with v.Fori(0, N_OVF - 1) as k:
                    with v.If(novf > k + 1):
                        v.wait_ge(S['silu'], k + 34)
                        v.scalar_tensor_tensor(act1, act1, 1.0, bank[2][:, 0:256], ALU.add, ALU.mult).then_inc(S['gated'], 1)
                        v.wait_ge(S['gated'], k + 34)
                        v.scalar_tensor_tensor(hact, act1, 0.5, bank[2][:, 256:512], ALU.mult, ALU.mult).then_inc(S['hact_ready'], 1)
                        v.wait_ge(S['dn_used'], k + 34)
                        v.tensor_copy(yb[0], bank[6][:, :]).then_inc(S['y_ready'], 1)
                        v.wait_ge(S['y_more'], k * 32 + 32)
                        v.nop().then_inc(S['v_go'], 1)
                    v.nop()
                v.nop()
            for t in range(T):
                r = ROWS[t]
                v.wait_ge(S[f'gath{t}'], 32)
                stt(x[0:r, t, :], yg[t][0][0:r, :], rt[0:r, RT_G1 + t:RT_G1 + t + 1], x[0:r, t, :], ALU.mult, ALU.add)
                v.scalar_tensor_tensor(x[0:r, t, :], yg[t][1][0:r, :], rt[0:r, RT_G2 + t:RT_G2 + t + 1], x[0:r, t, :],
                                       ALU.mult, ALU.add).then_inc(S['x3'], 1)


def kernel(**inputs):
    import concourse.bacc as bacc
    import concourse.mybir as mybir
    from concourse.bass_utils import run_bass_kernel_spmd

    nc = bacc.Bacc("TRN2", target_bir_lowering=False, num_devices=1)
    arrays, args = {}, {}
    for name in INS:
        arrays[f"in_{name}"] = np.ascontiguousarray(inputs[name])
    for name, a in CONSTS.items():
        arrays[f"in_{name}"] = a
    for name, a in arrays.items():
        args[name[3:]] = nc.dram_tensor(name, a.shape, mybir.dt.from_np(a.dtype), kind="ExternalInput").ap()
    for name, shape in OUTS:
        args[name] = nc.dram_tensor(f"out_{name}", shape, mybir.dt.float32, kind="ExternalOutput").ap()
    build(nc, args)
    r = run_bass_kernel_spmd(nc, [arrays], core_ids=[0])
    return tuple(r.results[0][f"out_{name}"] for name, _ in OUTS)
```
